# Optimizing a Trainium2 kernel written in Bass

```python
import jax, jax.numpy as jnp
from jax import lax
import numpy as np

D_MODEL = 1024
BATCH = 1
SEQ = 128
DEPTH = 2
DEC_BATCH = 1
DEC_SEQ = 512
PAST_LEN = 128

GRID_W = 64
HEAD_DIM = 64
N_HEADS = 8
N_KV_HEADS = 2
ATTN_WIDTH = N_HEADS * HEAD_DIM
KV_WIDTH = N_KV_HEADS * HEAD_DIM
POOL_WIDTH = D_MODEL - ATTN_WIDTH
POOL_WINDOWS = (2, 4, 8, 16)
N_POOL_GROUPS = 4
POOL_GROUP_DIM = POOL_WIDTH // N_POOL_GROUPS
IN_WIDTH = ATTN_WIDTH + 2 * KV_WIDTH + POOL_WIDTH
D_FF = 2816
CONV_WIDTH = 3
Q_BLOCK = 128
ROPE_THETA = 10000.0
EPS = 1e-6
N_MOD = 6

kernel_name = 'hybrid_attn_pool_diffusion_trunk'

def rms_norm(x, g):
    xf = x.astype(jnp.float32)
    y = xf * lax.rsqrt(jnp.mean(xf * xf, axis=-1, keepdims=True) + EPS)
    return (y * g.astype(jnp.float32)).astype(x.dtype)

def modulation(cond, w_mod, b_mod):
    m = jax.nn.silu(cond) @ w_mod + b_mod
    return jnp.split(m[:, None, :], N_MOD, axis=-1)

def axial_rope_tables(n_tokens):
    t = jnp.arange(n_tokens)
    row = (t // GRID_W).astype(jnp.float32)
    col = (t % GRID_W).astype(jnp.float32)
    n_freq = HEAD_DIM // 4
    inv = ROPE_THETA ** (-jnp.arange(n_freq, dtype=jnp.float32) / n_freq)
    ang = jnp.concatenate([row[:, None] * inv, col[:, None] * inv], axis=-1)
    return jnp.cos(ang), jnp.sin(ang)

def apply_axial_rope(x, cos, sin):
    b, l, h, d = x.shape
    xf = x.astype(jnp.float32).reshape(b, l, h, 2, 2, d // 4)
    x1, x2 = xf[..., 0, :], xf[..., 1, :]
    c = cos.reshape(l, 1, 2, d // 4)
    s = sin.reshape(l, 1, 2, d // 4)
    out = jnp.stack([x1 * c - x2 * s, x1 * s + x2 * c], axis=-2)
    return out.reshape(b, l, h, d).astype(x.dtype)

def block_attention(q, k, v):
    b, l, h, d = q.shape
    n_blk = l // Q_BLOCK
    grp = h // N_KV_HEADS
    qb = q.reshape(b, n_blk, Q_BLOCK, N_KV_HEADS, grp, d).transpose(1, 0, 2, 3, 4, 5)
    kf = k.astype(jnp.float32)
    vf = v.astype(jnp.float32)
    scale = d ** -0.5

    def one_block(qi):
        s = jnp.einsum('bqkgd,bskd->bkgqs', qi.astype(jnp.float32), kf) * scale
        p = jax.nn.softmax(s, axis=-1)
        return jnp.einsum('bkgqs,bskd->bqkgd', p, vf).astype(q.dtype)

    ob = lax.map(one_block, qb)
    return ob.transpose(1, 0, 2, 3, 4, 5).reshape(b, l, h * d)

def pool_mixer(u, w_pool, pool_scale):
    b, l, _ = u.shape
    ug = u.astype(jnp.float32).reshape(b, l, N_POOL_GROUPS, POOL_GROUP_DIM)
    csum = jnp.pad(jnp.cumsum(ug, axis=1), ((0, 0), (1, 0), (0, 0), (0, 0)))
    t = jnp.arange(l)
    outs = []
    for gi, w in enumerate(POOL_WINDOWS):
        lo = jnp.clip(t - w // 2, 0, l)
        hi = jnp.clip(t + (w - w // 2), 0, l)
        total = csum[:, hi, gi] - csum[:, lo, gi]
        cnt = (hi - lo).astype(jnp.float32)[None, :, None]
        outs.append(total / cnt - ug[:, :, gi])
    pooled = jnp.stack(outs, axis=2)
    mixed = jnp.einsum('blgc,gcd->blgd', pooled, w_pool.astype(jnp.float32))
    return (mixed.reshape(b, l, POOL_WIDTH) * pool_scale).astype(u.dtype)

def conv_ffn(h, w_up, conv_w, conv_b, w_down):
    z = h @ w_up
    zp = jnp.pad(z, ((0, 0), (1, 1), (0, 0)))
    z = zp[:, :-2] * conv_w[0] + zp[:, 1:-1] * conv_w[1] + zp[:, 2:] * conv_w[2] + conv_b
    a, g = jnp.split(z, 2, axis=-1)
    return (jax.nn.silu(a) * g) @ w_down

def mixer_projections(h, w_in, q_norm_g, k_norm_g):
    b, l, _ = h.shape
    proj = h @ w_in
    q, k, v, u = jnp.split(proj, [ATTN_WIDTH, ATTN_WIDTH + KV_WIDTH, ATTN_WIDTH + 2 * KV_WIDTH], axis=-1)
    q = rms_norm(q.reshape(b, l, N_HEADS, HEAD_DIM), q_norm_g)
    k = rms_norm(k.reshape(b, l, N_KV_HEADS, HEAD_DIM), k_norm_g)
    v = v.reshape(b, l, N_KV_HEADS, HEAD_DIM)
    return q, k, v, u

def trunk_layer(x, cond, ctx_k, ctx_v, p):
    sh1, sc1, gt1, sh2, sc2, gt2 = modulation(cond, p['w_mod'], p['b_mod'])
    h = rms_norm(x, p['norm1_g']) * (1.0 + sc1) + sh1
    q, k, v, u = mixer_projections(h, p['w_in'], p['q_norm_g'], p['k_norm_g'])
    if ctx_k is None:
        attn = block_attention(q, k, v)
        new_k, new_v = k, v
    else:
        cos, sin = axial_rope_tables(x.shape[1])
        q = apply_axial_rope(q, cos, sin)
        k = apply_axial_rope(k, cos, sin)
        keys = jnp.concatenate([ctx_k.astype(k.dtype), k], axis=1)
        vals = jnp.concatenate([ctx_v.astype(v.dtype), v], axis=1)
        attn = block_attention(q, keys, vals)
        new_k, new_v = None, None
    pooled = pool_mixer(u, p['w_pool'], p['pool_scale'])
    mix = jnp.concatenate([attn, pooled.astype(attn.dtype)], axis=-1) @ p['w_out']
    x = x + gt1 * mix
    h2 = rms_norm(x, p['norm2_g']) * (1.0 + sc2) + sh2
    x = x + gt2 * conv_ffn(h2, p['w_up'], p['conv_w'], p['conv_b'], p['w_down'])
    return x, new_k, new_v

def setup_inputs(seed: int = 0) -> dict:
    key = jax.random.key(seed)
    ks = jax.random.split(key, 24)
    nrm = jax.random.normal
    f32 = jnp.float32
    d = D_MODEL
    return {
        'x_prompt': nrm(ks[0], (BATCH, SEQ, d), f32),
        'x_sample': nrm(ks[1], (DEC_BATCH, DEC_SEQ, d), f32),
        'cache_k': nrm(ks[2], (DEC_BATCH, DEPTH, PAST_LEN, N_KV_HEADS, HEAD_DIM), f32),
        'cache_v': nrm(ks[3], (DEC_BATCH, DEPTH, PAST_LEN, N_KV_HEADS, HEAD_DIM), f32),
        'c': nrm(ks[4], (DEC_BATCH, d), f32),
        'c_ctx': nrm(ks[5], (d,), f32),
        'w_mod': nrm(ks[6], (DEPTH, d, N_MOD * d), f32) * (0.5 * d ** -0.5),
        'b_mod': nrm(ks[7], (DEPTH, N_MOD * d), f32) * 0.01,
        'norm1_g': 1.0 + 0.05 * nrm(ks[8], (DEPTH, d), f32),
        'w_in': nrm(ks[9], (DEPTH, d, IN_WIDTH), f32) * d ** -0.5,
        'q_norm_g': 1.0 + 0.05 * nrm(ks[10], (DEPTH, HEAD_DIM), f32),
        'k_norm_g': 1.0 + 0.05 * nrm(ks[11], (DEPTH, HEAD_DIM), f32),
        'w_pool': nrm(ks[12], (DEPTH, N_POOL_GROUPS, POOL_GROUP_DIM, POOL_GROUP_DIM), f32) * POOL_GROUP_DIM ** -0.5,
        'pool_scale': 1.0 + 0.05 * nrm(ks[13], (DEPTH, POOL_WIDTH), f32),
        'w_out': nrm(ks[14], (DEPTH, d, d), f32) * d ** -0.5,
        'norm2_g': 1.0 + 0.05 * nrm(ks[15], (DEPTH, d), f32),
        'w_up': nrm(ks[16], (DEPTH, d, 2 * D_FF), f32) * d ** -0.5,
        'conv_w': nrm(ks[17], (DEPTH, CONV_WIDTH, 2 * D_FF), f32) * CONV_WIDTH ** -0.5,
        'conv_b': nrm(ks[18], (DEPTH, 2 * D_FF), f32) * 0.01,
        'w_down': nrm(ks[19], (DEPTH, D_FF, d), f32) * D_FF ** -0.5,
        'final_norm_g': 1.0 + 0.05 * nrm(ks[20], (d,), f32),
    }

def reference(x_prompt, x_sample, cache_k, cache_v, c, c_ctx, w_mod, b_mod, norm1_g, w_in,
              q_norm_g, k_norm_g, w_pool, pool_scale, w_out, norm2_g, w_up, conv_w, conv_b,
              w_down, final_norm_g):
    cond_ctx = c_ctx[None, :]
    xp = x_prompt
    xs = x_sample
    ks_out = []
    vs_out = []
    for i in range(DEPTH):
        p = {'w_mod': w_mod[i], 'b_mod': b_mod[i], 'norm1_g': norm1_g[i], 'w_in': w_in[i],
             'q_norm_g': q_norm_g[i], 'k_norm_g': k_norm_g[i], 'w_pool': w_pool[i],
             'pool_scale': pool_scale[i], 'w_out': w_out[i], 'norm2_g': norm2_g[i],
             'w_up': w_up[i], 'conv_w': conv_w[i], 'conv_b': conv_b[i], 'w_down': w_down[i]}
        xp, k_i, v_i = trunk_layer(xp, cond_ctx, None, None, p)
        ks_out.append(k_i)
        vs_out.append(v_i)
        xs, _, _ = trunk_layer(xs, c, cache_k[:, i], cache_v[:, i], p)
    y_prompt = rms_norm(xp, final_norm_g)
    y_sample = rms_norm(xs, final_norm_g)
    new_cache_k = jnp.stack(ks_out, axis=1)
    new_cache_v = jnp.stack(vs_out, axis=1)
    return (y_prompt, y_sample, new_cache_k, new_cache_v)


_drawn_inputs = setup_inputs


def setup_inputs(seed=0):
    import zlib

    import numpy as np

    out = dict(_drawn_inputs(seed))
    spreads = {}
    factors = {'cache_k': 8.0,
     'cache_v': 6.665,
     'b_mod': 3.696,
     'q_norm_g': 8.0,
     'pool_scale': 3.926,
     'conv_b': 8.0}
    for name, (base, spread) in spreads.items():
        noise = np.random.default_rng([zlib.crc32(name.encode()), seed]).standard_normal(out[name].shape)
        drawn = base * np.exp(spread * noise) if base else spread * noise
        out[name] = __import__('jax').numpy.asarray(drawn.astype(out[name].dtype))
    for name, factor in factors.items():
        out[name] = (out[name] * factor).astype(out[name].dtype)
    return out
```

```python
from contextlib import ExitStack

import numpy as np

import concourse.bass as bass
from concourse import mybir

F32 = mybir.dt.float32
F32R = mybir.dt.float32r
ALU = mybir.AluOpType
ACT = mybir.ActivationFunctionType
AX_X = mybir.AxisListType.X

P = 128
HALF = P // 2
EPS = 1e-6
GRID_W = 64
ROPE_THETA = 10000.0
WINDOWS = (2, 4, 8, 16)
PAD = max(WINDOWS) // 2


def ds(start, size):
    return bass.ds(start, size)


def shape_constants(n_prompt, n_sample, head_dim):
    ident = np.eye(P, dtype=np.float32)
    block = np.kron(np.eye(P // head_dim), np.ones((head_dim, head_dim))).astype(np.float32)
    ones = np.ones((P, P), np.float32)
    quarter = head_dim // 4
    inv = (np.float32(ROPE_THETA) ** (-np.arange(quarter, dtype=np.float32) / np.float32(quarter))).astype(np.float32)
    t = np.arange(n_sample)
    where = np.stack([t // GRID_W, t % GRID_W]).astype(np.float32)
    d = np.arange(P) % head_dim
    axis, second, freq = d // (2 * quarter), (d // quarter) % 2, d % quarter
    angle = (where[axis] * inv[freq][:, None]).astype(np.float32)
    sign = np.where(second == 1, 1.0, -1.0)[:, None]
    edges = np.ones((len(WINDOWS), 2, 2, PAD), np.float32)
    for g, w in enumerate(WINDOWS):
        for s, n in enumerate((n_prompt, n_sample)):
            at = np.concatenate([np.arange(PAD), np.arange(n - PAD, n)])
            count = np.clip(at + w - w // 2, 0, n) - np.clip(at - w // 2, 0, n)
            edges[g, s] = (w / count).reshape(2, PAD)
    return np.concatenate([
        ident, block, ones, np.cos(angle), (np.sin(angle) * sign),
        np.broadcast_to(edges.reshape(1, -1), (P, edges.size))], axis=1).astype(np.float32)


def build(nc, x_prompt, x_sample, cache_k, cache_v, c, c_ctx, w_mod, b_mod, norm1_g, w_in,
          q_norm_g, k_norm_g, w_pool, pool_scale, w_out, norm2_g, w_up, conv_w, conv_b,
          w_down, final_norm_g, consts, y_prompt, y_sample, new_k, new_v):
    DEPTH, D, IN_WIDTH = w_in.shape
    TP, TS = x_prompt.shape[1], x_sample.shape[1]
    T = TP + TS
    HALF_T = T // 2
    PAST = cache_k.shape[2]
    HD = cache_k.shape[4]
    KV = cache_k.shape[3] * HD
    NPOOL = w_pool.shape[1]
    AW = D - NPOOL * P
    NH = AW // HD
    GRP = NH // cache_k.shape[3]
    FF = w_down.shape[1]
    NK = D // P
    NT = T // P
    NQ = AW // P
    NF = FF // P
    NG = 2
    FG = NF // NG
    N_MOD = 6
    SCALE = float(HD) ** -0.5
    assert TP == P and TS % P == 0 and KV == P and PAST == P and NF % NG == 0 and HALF_T % 2 == 0
    SEG = ((0, 0, TP), (1, TP, T))

    N_IN, N_OUT = IN_WIDTH // P, NK
    PER_GROUP = 2 * FG + NK
    PER_LAYER = N_IN + N_OUT + NG * PER_GROUP
    IN_K, IN_V, IN_Q, IN_U = 0, 1, 2, 2 + NQ
    IN_COLUMN = [AW, AW + KV] + [P * t for t in range(NQ)] + [AW + 2 * KV + P * g for g in range(NPOOL)]

    def tile_in(L):
        return L * PER_LAYER

    def tile_out(L):
        return tile_in(L) + N_IN

    def tile_up(L, g):
        return tile_out(L) + N_OUT + g * PER_GROUP

    def tile_down(L, g):
        return tile_up(L, g) + 2 * FG

    UNITS = [(b, h) for b in range(NT) for h in range(NH)]
    NU = len(UNITS)

    with ExitStack() as ctx:
        def sb(name, shape, dt=F32, at=ctx):
            return at.enter_context(nc.sbuf_tensor(name, shape, dt))

        def sem(name):
            return ctx.enter_context(nc.semaphore(name))

        x = sb("x", [P, NK, T])
        in_hi = sb("in_hi", [P, NK, T], F32R)
        in_lo = sb("in_lo", [P, NK, T], F32R)
        w_raw = sb("w_raw", [P, 2, FG, P])
        w_hi = sb("w_hi", [P, 2, FG, P], F32R)
        w_lo = sb("w_lo", [P, 2, FG, P], F32R)
        mod_raw = sb("mod_raw", [P, 2, D])
        mod_acc = sb("mod_acc", [P, 2, 2, D])
        n_const = consts.shape[1]
        cst = sb("cst", [P, n_const])
        ident, head_ones, ones = (cst[:, i * P:(i + 1) * P] for i in range(3))
        cos, sin = (cst[:, 3 * P + i * TS:3 * P + (i + 1) * TS] for i in range(2))
        edge = cst[:, 3 * P + 2 * TS:n_const].rearrange("p (g s e c) -> p g s e c", g=NPOOL, s=2, e=2)
        vec = sb("vec", [P, DEPTH, 3, P])
        mod = sb("mod", [P, DEPTH, N_MOD, 2, NK])
        gain = sb("gain", [P, DEPTH, 2, 2, NK])
        cond = sb("cond", [P, 2, NK])
        eps = sb("eps", [P, 1])
        wp = sb("wp", [P, NPOOL, P])
        past = sb("past", [P, 2, P])
        val = sb("val", [P, NT, P])
        k_out = sb("k_out", [P, P])
        sq = sb("sq", [P, 2, T])
        ssum = sb("ssum", [P, T])
        rstd = sb("rstd", [P, T])
        small = sb("small", [P, 2, 4])

        with ExitStack() as own:
            xin = sb("xin", [P, NT, D], at=own)
            rows = sb("rows", [P, DEPTH, 3, P], at=own)
        with ExitStack() as own:
            yf = sb("yf", [P, NK, T], at=own)
            yout = sb("yout", [P, NT, D], at=own)
        with ExitStack() as own:
            norm_t = sb("norm_t", [P, 2, T], at=own)
        with ExitStack() as own:
            q = sb("q", [P, NQ, T], at=own)
            qk_raw = sb("qk_raw", [P, 2, T], at=own)
            qk_rstd = sb("qk_rstd", [P, 2, T], at=own)
            keys = sb("keys", [P, T + PAST], at=own)
            keys_x = sb("keys_x", [P, T + PAST], at=own)
            rope = sb("rope", [P, 2, TS], at=own)
            v_feat = sb("v_feat", [P, T], at=own)
            prob = sb("prob", [P, 2, T], at=own)
            prob_t = sb("prob_t", [P, 2, T], at=own)
            U_P, U_S = PAD, TP + 2 * PAD
            U_W = U_S + TS + PAD
            u = sb("u", [P, NPOOL, U_W], at=own)
            tree = sb("tree", [P, 2, U_W], at=own)
        with ExitStack() as own:
            conv = sb("conv", [P, 2, T], at=own)
            act_hi = sb("act_hi", [P, FG, T], F32R, at=own)
            act_lo = sb("act_lo", [P, FG, T], F32R, at=own)
            silu_a = sb("silu_a", [P, T], at=own)

        pair = [ctx.enter_context(nc.psum_tensor(f"pair{i}", [P, 2 * 512], F32)) for i in range(4)]
        LIN0 = 512 - HALF_T
        lin = [pair[i][:, LIN0:LIN0 + T] for i in range(4)]
        MODP = 832
        n_red = 2 * NK

        V_BMOD, V_CONVB, V_N1, V_N2, V_PS, V_QG, V_KG = (0, 0), (0, 48), (0, 92), (0, 100), (0, 108), (0, 112), (0, 113)
        V_TAP = ((1, 0), (1, NF * 2), (2, 0))
        V_FIN, V_CTX, V_C = (2, 44), (2, 52), (2, 60)
        N_ROWS = (114, 88, 68)
        assert 2 * NF == 44 and NK == 8

        def v(L, place, i, n=1):
            return vec[:, L, place[0], ds(place[1] + i, n)]

        s_const, s_rows, s_x = sem("const_loaded"), sem("rows_loaded"), sem("x_loaded")
        s_vec_t, s_vec = sem("vec_transposed"), sem("vec_ready")
        s_cond, s_eps = sem("cond_ready"), sem("eps_ready")
        s_xt, s_xe = sem("x_transposed"), sem("x_evacuated")
        s_raw = [sem(f"w_loaded{i}") for i in range(2)]
        s_whi, s_wlo = sem("w_hi_ready"), sem("w_lo_ready")
        s_lin, s_free = sem("lin_done"), sem("lin_free")
        s_gain = sem("gain_ready")
        s_mraw = [sem(f"mod_loaded{i}") for i in range(2)]
        s_macc, s_mred, s_mod = sem("mod_accumulated"), sem("mod_reduced"), sem("mod_ready")
        s_xupd, s_sq, s_ss, s_ss0 = sem("x_updated"), sem("squares_ready"), sem("squares_summed"), sem("sum_cleared")
        s_stat, s_sd, s_rstd = sem("stat_done"), sem("std_ready"), sem("rstd_ready")
        s_nt, s_hhi, s_h = sem("normed"), sem("h_hi_ready"), sem("h_ready")
        s_qsq, s_qst, s_qsd, s_qrs = sem("qk_squared"), sem("qk_stat"), sem("qk_std"), sem("qk_rstd_ready")
        s_qraw, s_qn, s_shuf = sem("qk_copied"), sem("qk_normed"), sem("qk_shuffled")
        s_rp, s_qk = sem("rope_part"), sem("qk_ready")
        s_vf, s_vt, s_val, s_pkt, s_pk = sem("v_copied"), sem("v_transposed"), sem("values_ready"), sem("past_transposed"), sem("past_key_ready")
        s_kt, s_kout, s_kx = sem("new_key_transposed"), sem("new_key_copied"), sem("keys_swapped")
        s_past, s_wp = sem("past_loaded"), sem("w_pool_loaded")
        s_out = sem("outputs_written")
        s_upad, s_u, s_tree, s_tstep, s_pooled = sem("pads_cleared"), sem("u_ready"), sem("window_sums"), sem("tree_step"), sem("pooled")
        s_pm, s_phi, s_plo = sem("pool_mixed"), sem("pool_hi"), sem("pool_lo")
        s_s, s_max, s_neg, s_exp, s_rec, s_prob = sem("scores_done"), sem("max_ready"), sem("neg_max_ready"), sem("exp_done"), sem("reciprocal_ready"), sem("prob_ready")
        s_pt, s_pte, s_o, s_ohi, s_olo = sem("prob_transposed"), sem("prob_t_ready"), sem("head_done"), sem("o_hi"), sem("o_lo")
        s_ctr, s_tap, s_silu = sem("conv_centre"), sem("conv_tap"), sem("silu_ready")
        s_act, s_ahi, s_alo = sem("act_ready"), sem("act_hi_ready"), sem("act_lo_ready")
        s_y, s_yt, s_ye = sem("y_ready"), sem("y_transposed"), sem("y_copied")

        block = ctx.enter_context(nc.Block())

        w_in_v = [w_in[L].rearrange("(k p) n -> p k n", p=P) for L in range(DEPTH)]
        w_out_v = [w_out[L].rearrange("(k p) n -> p k n", p=P) for L in range(DEPTH)]
        w_up_v = [w_up[L].rearrange("(k p) n -> p k n", p=P) for L in range(DEPTH)]
        w_down_v = [w_down[L].rearrange("(k p) n -> p k n", p=P) for L in range(DEPTH)]

        def mod_slot(L, pr, k):
            return (L * 3 + pr) * NK + k

        def o_bank(b):
            return pair[3][:, (b % 2) * 512:(b % 2) * 512 + NQ * P].rearrange("p (t c) -> p t c", t=NQ)

        def y_bank(i):
            return pair[i % 8 // 2][:, (i % 2) * 512:(i % 2) * 512 + 512]

        def upd_out(L):
            return L * (1 + NG) * NK

        def upd_down(L, g):
            return upd_out(L) + (1 + g) * NK

        
        @block.sync
        def _(sp):
            def load_w(n, s, src, nk):
                if not isinstance(n, int) or n >= 2:
                    sp.wait_ge(s_wlo, n - 1)
                sp.dma_start(w_raw[:, s, 0:nk, :], src).then_inc(s_raw[s], 16)

            def load_mod(L, pr, k):
                for i in range(2):
                    before = mod_slot(L, pr, k)
                    if not isinstance(before, int) or before >= 1:
                        sp.wait_ge(s_macc, 4 * before - 2 + 2 * i)
                    col = (2 * pr + i) * D
                    sp.dma_start(mod_raw[:, i, :], w_mod[L, ds(k * P, P), col:col + D]).then_inc(s_mraw[i], 16)

            for src, at, n, t in ((b_mod, 0, 48, 0), (conv_b, 48, 44, 0), (norm1_g, 92, NK, 0), (norm2_g, 100, NK, 0),
                                  (pool_scale, 108, NPOOL, 0)):
                sp.dma_start(rows[at:at + n, :, t, :], src.rearrange("l (r c) -> r l c", c=P)).then_inc(s_rows, 16)
            for src, at in ((q_norm_g, 112), (k_norm_g, 113)):
                for i in range(2):
                    sp.dma_start(rows[at:at + 1, :, 0, i * HD:(i + 1) * HD],
                                 src.rearrange("l (r c) -> r l c", r=1)).then_inc(s_rows, 16)
            for tap, (t, at) in enumerate(V_TAP):
                sp.dma_start(rows[at:at + 2 * NF, :, t, :],
                             conv_w[:, tap, :].rearrange("l (r c) -> r l c", c=P)).then_inc(s_rows, 16)
            for L in range(DEPTH):
                for src, at in ((final_norm_g, 44), (c_ctx, 52), (c.rearrange("a d -> (a d)"), 60)):
                    sp.dma_start(rows[at:at + NK, L, 2, :], src.rearrange("(r c) -> r c", c=P)).then_inc(s_rows, 16)
            for k in range(2):
                load_mod(0, 0, k) if k == 0 else None
            for n in range(2):
                load_w(n, n, w_in_v[0][:, :, IN_COLUMN[n]:IN_COLUMN[n] + P], NK)
            for k in range(1, NK):
                load_mod(0, 0, k)
            for n in range(2, 4):
                load_w(n, n % 2, w_in_v[0][:, :, IN_COLUMN[n]:IN_COLUMN[n] + P], NK)
            for L in range(DEPTH):
                load_mod(L, 1, 0)
                if L > 0:
                    sp.wait_ge(s_pm, L * NPOOL)
                sp.dma_start(past[:, 0, :], cache_k[0, L].rearrange("t h d -> t (h d)")).then_inc(s_past, 16)
                sp.dma_start(past[:, 1, :], cache_v[0, L].rearrange("t h d -> t (h d)")).then_inc(s_past, 16)
                sp.dma_start(wp[:, :, :], w_pool[L].rearrange("g c d -> c g d")).then_inc(s_wp, 16)
                for n in range(4, N_IN):
                    load_w(tile_in(L) + n, n % 2, w_in_v[L][:, :, IN_COLUMN[n]:IN_COLUMN[n] + P], NK)
                    if n - 3 < NK:
                        load_mod(L, 1, n - 3)
                for m in range(4):
                    load_w(tile_out(L) + m, m % 2, w_out_v[L][:, :, m * P:(m + 1) * P], NK)
                    if m + N_IN - 3 < NK:
                        load_mod(L, 1, m + N_IN - 3)
                for k in range(NK):
                    load_mod(L, 2, k)
                for m in range(4, N_OUT):
                    load_w(tile_out(L) + m, m % 2, w_out_v[L][:, :, m * P:(m + 1) * P], NK)
                for g in range(NG):
                    mods = g == 0 and L + 1 < DEPTH

                    def load_up(j, L=L, g=g):
                        for s in range(2):
                            load_w(tile_up(L, g) + 2 * j + s, s,
                                   w_up_v[L][:, :, ds(s * FF + (g * FG + j) * P, P)], NK)
                    if mods:
                        load_up(0)
                        load_mod(L + 1, 0, 0)
                        load_up(1)
                        with sp.Fori(2, NK + 1) as j:
                            load_up(j)
                            load_mod(L + 1, 0, j - 1)
                        with sp.Fori(NK + 1, FG) as j:
                            load_up(j)
                    else:
                        with sp.Fori(0, FG) as j:
                            load_up(j)
                    with sp.Fori(0, NK // 2) as i:
                        for s in range(2):
                            load_w(tile_down(L, g) + 2 * i + s, s,
                                   w_down_v[L][:, g * FG:(g + 1) * FG, ds((2 * i + s) * P, P)], FG)
                if L + 1 < DEPTH:
                    for n in range(4):
                        load_w(tile_in(L + 1) + n, n % 2,
                               w_in_v[L + 1][:, :, IN_COLUMN[n]:IN_COLUMN[n] + P], NK)
            for b in range(NT):
                sp.wait_ge(s_ye, 2 * (b + 1))
                dst = y_prompt[0] if b == 0 else y_sample[0, (b - 1) * P:b * P, :]
                sp.dma_start(dst, yout[:, b, :]).then_inc(s_out, 16)
            sp.wait_ge(s_out, 16 * (NT + 2 * DEPTH))

        @block.gpsimd
        def _(pool):
            pool.memset(eps[:, :], EPS).then_inc(s_eps, 1)

            def clear_sum(i):
                if i > 0:
                    pool.wait_ge(s_stat, i)
                pool.memset(ssum[:, :], 0.0).then_inc(s_ss0, 1)

            def add_squares(i, base, m):
                if isinstance(m, int) and m == 0:
                    pool.wait_ge(s_ss0, i + 1)
                else:
                    pool.wait_ge(s_ss, base + m)
                pool.wait_ge(s_sq, base + m + 1)
                pool.tensor_tensor(ssum[:, :], ssum[:, :], sq_slot(m), ALU.add).then_inc(s_ss, 1)

            def sq_slot(m):
                return sq[:, m % 2, :]

            clear_sum(0)
            for m in range(NK):
                add_squares(0, 0, m)
            for L in range(DEPTH):
                if L > 0:
                    pool.wait_ge(s_lin, tile_in(L))
                else:
                    pool.wait_ge(s_xe, NK)
                    pool.wait_ge(s_vec, DEPTH)
                for at in (0, U_P + TP, U_S + TS):
                    pool.memset(u[:, :, at:at + PAD], 0.0).then_inc(s_upad, 1)
                for e in range(1 + NQ):
                    E = L * (1 + NQ) + e
                    tgt = keys[:, TP + PAST:TP + PAST + TS] if e == 0 else q[:, e - 1, TP:T]
                    if E > 0:
                        pool.wait_ge(s_qk, E)
                    pool.wait_ge(s_shuf, E + 1)
                    pool.tensor_tensor(rope[:, 1, :], rope[:, 0, :], sin, ALU.mult).then_inc(s_rp, 1)
                    pool.tensor_tensor(tgt, tgt, cos, ALU.mult).then_inc(s_rp, 1)
                    pool.wait_ge(s_rp, 2 * E + 2)
                    pool.tensor_tensor(tgt, tgt, rope[:, 1, :], ALU.add).then_inc(s_qk, 1)
                done = L * sum(range(1, NPOOL + 1))
                pool.wait_ge(s_upad, 3 * (L + 1))
                for g in range(NPOOL):
                    pool.wait_ge(s_u, 2 * (L * NPOOL + g + 1))
                    src, lo, hi = u[:, g, :], 0, U_W
                    for r in range(g + 1):
                        left, right = (1, 0) if r == 0 else (2 ** (r - 1), 2 ** (r - 1))
                        lo, hi = lo + left, hi - right
                        dst = tree[:, r % 2, :]
                        if r == 0 and L * NPOOL + g > 0:
                            pool.wait_ge(s_pooled, L * NPOOL + g)
                        if r > 0:
                            pool.wait_ge(s_tstep, done)
                        pool.tensor_tensor(dst[:, lo:hi], src[:, lo - left:hi - left], src[:, lo + right:hi + right],
                                           ALU.add).then_inc(s_tstep, 1)
                        done += 1
                        src = dst
                    pool.wait_ge(s_tstep, done)
                    for s, (at, n) in enumerate(((U_P, TP), (U_S, TS))):
                        for e_, a0 in enumerate((at, at + n - PAD)):
                            pool.tensor_tensor(src[:, a0:a0 + PAD], src[:, a0:a0 + PAD], edge[:, g, s, e_, :],
                                               ALU.mult).then_inc(s_tree, 1)
                clear_sum(2 * L + 1)
                base = (2 * L + 1) * NK
                for m in range(NK):
                    add_squares(2 * L + 1, base, m)
                for g in range(NG):
                    def gate(j, L=L, g=g):
                        n = (L * NG + g) * FG + j
                        pool.wait_ge(s_silu, n + 1)
                        pool.wait_ge(s_tap, 8 * n + 8)
                        pool.tensor_tensor(silu_a[:, :], silu_a[:, :], conv[:, 1, :], ALU.mult).then_inc(s_act, 1)
                        pool.wait_ge(s_act, n + 1)
                        pool.tensor_copy(act_hi[:, j, :], silu_a[:, :]).then_inc(s_ahi, 1)
                        pool.wait_ge(s_ahi, n + 1)
                        pool.tensor_tensor(act_lo[:, j, :], silu_a[:, :], act_hi[:, j, :].bitcast(F32),
                                           ALU.subtract).then_inc(s_alo, 1)
                    with pool.Fori(0, FG) as j:
                        gate(j)
                clear_sum(2 * L + 2)
                base = (2 * L + 2) * NK
                for m in range(NK):
                    add_squares(2 * L + 2, base, m)

        @block.scalar
        def _(act_e):
            def hi(n, s, nk):
                act_e.wait_ge(s_raw[s], 16 * slot_loads(n, s))
                if not isinstance(n, int) or n >= 2:
                    act_e.wait_ge(s_lin, n - 1)
                act_e.activation(w_hi[:, s, 0:nk, :], w_raw[:, s, 0:nk, :], ACT.Copy).then_inc(s_whi, 1)

            def slot_loads(n, s):
                return n // 2 + 1 if isinstance(n, int) else (n - s) // 2 + 1

            def hi_at(base, i, s, nk):
                act_e.wait_ge(s_raw[s], 16 * (i + (base // 2 + 1)))
                act_e.wait_ge(s_lin, 2 * i + (base + s - 1))
                act_e.activation(w_hi[:, s, 0:nk, :], w_raw[:, s, 0:nk, :], ACT.Copy).then_inc(s_whi, 1)

            def squares(count, upd, m):
                act_e.wait_ge(s_xupd, upd)
                if not isinstance(count, int) or count >= 2:
                    act_e.wait_ge(s_ss, count - 1)
                act_e.activation(sq[:, m % 2, :], x[:, m, :], ACT.Square).then_inc(s_sq, 1)

            def norm(i, L, which):
                act_e.wait_ge(s_stat, i + 1)
                if i > 0:
                    act_e.wait_ge(s_nt, i * NK * 2)
                act_e.activation(rstd[:, :], lin[3], ACT.Sqrt, bias=eps[:, :], scale=1.0 / D).then_inc(s_sd, 1)
                if L is None:
                    return
                for k in range(NK):
                    for ci, a, b in SEG:
                        act_e.wait_ge(s_nt, 2 * (i * NK + k) + 1 + ci)
                        act_e.activation(in_hi[:, k, a:b], norm_t[:, k % 2, a:b], ACT.Identity,
                                         bias=mod[:, L, 3 * which, ci, k:k + 1]).then_inc(s_hhi, 1)

            act_e.dma_start(cst[:, :], consts).then_inc(s_const, 16)
            act_e.dma_start(xin[:, 0, :], x_prompt[0]).then_inc(s_x, 16)
            act_e.dma_start(xin[:, 1:NT, :], x_sample[0].rearrange("(t p) d -> p t d", p=P)).then_inc(s_x, 16)
            for L in range(DEPTH):
                act_e.wait_ge(s_vec_t, L + 1)
                for t in range(3):
                    ins = act_e.activation(vec[:, L, t, 0:N_ROWS[t]], pair[2][:, t * P:t * P + N_ROWS[t]], ACT.Copy)
                ins.then_inc(s_vec, 1)
            act_e.wait_ge(s_vec, 1)
            act_e.activation(cond[:, :, :].rearrange("p a b -> p (a b)"), vec[:, 0, 2, 52:52 + 2 * NK], ACT.Silu).then_inc(s_cond, 1)
            for n in range(2):
                hi(n, n, NK)
            for k in range(NK):
                act_e.wait_ge(s_xt, k + 1)
                act_e.activation(x[:, k, :], pair[k % 2][:, 0:T], ACT.Copy).then_inc(s_xe, 1)
                act_e.wait_ge(s_xe, k + 1)
                if k >= 2:
                    act_e.wait_ge(s_ss, k - 1)
                act_e.activation(sq[:, k % 2, :], x[:, k, :], ACT.Square).then_inc(s_sq, 1)
            act_e.wait_ge(s_eps, 1)
            for L in range(DEPTH):
                act_e.wait_ge(s_mod, L * N_MOD + 2)
                norm(2 * L, L, 0)
                for n in range(N_IN):
                    N = tile_in(L) + n
                    act_e.wait_ge(s_lin, N + 1)
                    e = 0 if n == IN_K else n - IN_Q + 1 if IN_Q <= n < IN_U else None
                    if e is not None:
                        E = L * (1 + NQ) + e
                        if e >= 2:
                            act_e.wait_ge(s_qst, E - 1)
                        else:
                            act_e.wait_ge(s_ss, (2 * L + 1) * NK)
                        act_e.activation(sq[:, E % 2, :], lin[n % 2], ACT.Square).then_inc(s_qsq, 1)
                    hi(N + 2, n % 2, NK)
                    e = 0 if n - 1 == IN_K else n - IN_Q if IN_Q <= n - 1 < IN_U else None
                    if e is not None:
                        E = L * (1 + NQ) + e
                        act_e.wait_ge(s_qst, E + 1)
                        if e >= 2:
                            act_e.wait_ge(s_qn, 2 * (E - 1))
                        act_e.activation(qk_rstd[:, e % 2, :], lin[3], ACT.Sqrt, bias=eps[:, :],
                                         scale=1.0 / HD).then_inc(s_qsd, 1)
                    if n == IN_Q:
                        act_e.wait_ge(s_vt, L + 1)
                        if L > 0:
                            act_e.wait_ge(s_out, 16 * 2 * L)
                            act_e.wait_ge(s_o, L * NU)
                        act_e.activation(val[:, :, :], pair[2][:, 0:T].rearrange("p (t c) -> p t c", t=NT),
                                         ACT.Copy).then_inc(s_val, 1)
                        act_e.activation(keys[:, TP:TP + PAST], pair[2][:, T:T + P], ACT.Copy).then_inc(s_pk, 1)
                        act_e.wait_ge(s_val, L + 1)
                        act_e.dma_start(new_v[0, L].rearrange("t h d -> t (h d)"), val[:, 0, :]).then_inc(s_out, 16)
                    if n == IN_Q + 3:
                        act_e.wait_ge(s_kt, L + 1)
                        act_e.activation(k_out[:, :], pair[2][:, T:T + P], ACT.Copy).then_inc(s_kout, 1)
                        act_e.wait_ge(s_kout, L + 1)
                        act_e.dma_start(new_k[0, L].rearrange("t h d -> t (h d)"), k_out[:, :]).then_inc(s_out, 16)
                        act_e.wait_ge(s_qk, L * (1 + NQ) + 1)
                        act_e.wait_ge(s_pk, L + 1)
                        for a in (0, HALF):
                            act_e.activation(keys_x[a:a + HALF, :], keys[HALF - a:P - a, :], ACT.Copy).then_inc(s_kx, 1)
                for i in range(NU + 2):
                    if i < NU:
                        un = L * NU + i
                        b, h = UNITS[i]
                        nkeys = P if b == 0 else T
                        act_e.wait_ge(s_neg, un + 1)
                        if i >= 2:
                            act_e.wait_ge(s_pt, un - 1)
                        act_e.activation(prob[:, i % 2, 0:nkeys], lin[i % 2][:, 0:nkeys], ACT.Exp,
                                         bias=small[:, i % 2, 0:1], scale=SCALE,
                                         accum_out=small[:, i % 2, 1:2]).then_inc(s_exp, 1)
                    if 1 <= i <= NU:
                        un = L * NU + i - 1
                        nkeys = P if UNITS[i - 1][0] == 0 else T
                        act_e.wait_ge(s_pt, un + 1)
                        if i - 1 >= 2:
                            act_e.wait_ge(s_o, un - 1)
                        act_e.activation(prob_t[:, (i - 1) % 2, 0:nkeys], pair[2][:, 0:nkeys],
                                         ACT.Copy).then_inc(s_pte, 1)
                    if i >= 2 and (i - 1) % NH == 0:
                        b = (i - 1) // NH - 1
                        act_e.wait_ge(s_o, L * NU + (b + 1) * NH)
                        act_e.activation(in_hi[:, 0:NQ, b * P:(b + 1) * P], o_bank(b), ACT.Copy).then_inc(s_ohi, 1)
                for g in range(NPOOL):
                    act_e.wait_ge(s_pm, L * NPOOL + g + 1)
                    act_e.activation(in_hi[:, NQ + g, :], lin[g % 2], ACT.Copy,
                                     scale=v(L, V_PS, g)).then_inc(s_phi, 1)
                up = tile_up(L, 0)
                out = tile_out(L)
                for m in range(N_OUT):
                    N = out + m
                    act_e.wait_ge(s_lin, N + 1)
                    hi(N + 2, m % 2, NK)
                    squares((2 * L + 1) * NK + m, upd_out(L) + m + 1, m)
                norm(2 * L + 1, L, 1)
                act_e.preload_act_table(ACT.Silu)
                for g in range(NG):
                    def up_iter(j, nxt, nk, L=L, g=g):
                        n = (L * NG + g) * FG + j
                        base = tile_up(L, g)
                        for s in range(2):
                            act_e.wait_ge(s_lin, 2 * j + (base + s + 1))
                            if L + g > 0 or not isinstance(j, int) or j > 0:
                                if s == 0:
                                    act_e.wait_ge(s_silu, n)
                                else:
                                    act_e.wait_ge(s_act, n)
                            act_e.activation(conv[:, s, :], lin[s], ACT.Identity, bias=v(L, V_CONVB, s * NF + g * FG + j),
                                             scale=v(L, V_TAP[1], s * NF + g * FG + j)).then_inc(s_ctr, 1)
                            if isinstance(nxt, int):
                                hi(nxt + s, s, nk)
                            else:
                                hi_at(base + 2, j, s, nk)
                        act_e.wait_ge(s_tap, 8 * n + 4)
                        if L + g > 0 or not isinstance(j, int) or j > 0:
                            act_e.wait_ge(s_alo, n)
                        act_e.activation(silu_a[:, :], conv[:, 0, :], ACT.Silu).then_inc(s_silu, 1)
                    up_iter(0, tile_up(L, g) + 2, NK)
                    with act_e.Fori(1, FG - 1) as j:
                        up_iter(j, None, NK)
                    up_iter(FG - 1, tile_down(L, g), FG)

                    last = g == NG - 1 and L == DEPTH - 1
                    down = tile_down(L, g)
                    for m in range(NK):
                        N = down + m
                        act_e.wait_ge(s_lin, N + 1)
                        if N + 2 < DEPTH * PER_LAYER:
                            hi(N + 2, m % 2, FG if m + 2 < NK else NK)
                        if g == NG - 1:
                            squares((2 * L + 2) * NK + m, upd_down(L, g) + m + 1, m)
            norm(2 * DEPTH, None, None)
            for b in range(NT):
                act_e.wait_ge(s_yt, 2 * b + 1)
                act_e.activation(yout[:, b, 0:512], y_bank(2 * b), ACT.Copy).then_inc(s_ye, 1)
                act_e.wait_ge(s_yt, 2 * b + 2)
                act_e.activation(yout[:, b, 512:1024], y_bank(2 * b + 1), ACT.Copy).then_inc(s_ye, 1)

        @block.vector
        def _(dve):
            def o_low(L, b):
                dve.wait_ge(s_ohi, L * NT + b + 1)
                dve.tensor_tensor(in_lo[:, 0:NQ, b * P:(b + 1) * P], o_bank(b),
                                  in_hi[:, 0:NQ, b * P:(b + 1) * P].bitcast(F32), ALU.subtract).then_inc(s_olo, 1)

            def lo(n, s, nk):
                dve.wait_ge(s_whi, n + 1)
                dve.tensor_tensor(w_lo[:, s, 0:nk, :], w_raw[:, s, 0:nk, :], w_hi[:, s, 0:nk, :].bitcast(F32),
                                  ALU.subtract).then_inc(s_wlo, 1)

            def mod_unit(L, pr, k, i):
                before = mod_slot(L, pr, k)
                dve.wait_ge(s_mraw[i], 16 * (before + 1))
                first = isinstance(k, int) and k == 0
                if first and L * 3 + pr > 0:
                    dve.wait_ge(s_mred, (L * 3 + pr) * 2)
                for ci in range(2):
                    if first:
                        dve.tensor_scalar(mod_acc[:, i, ci, :], mod_raw[:, i, :], cond[:, ci, 0:1], None,
                                          ALU.mult).then_inc(s_macc, 1)
                    else:
                        dve.wait_ge(s_macc, 4 * before + (2 * i + ci + 1 - 4))
                        dve.scalar_tensor_tensor(out=mod_acc[:, i, ci, :], in0=mod_raw[:, i, :],
                                                 scalar=cond[:, ci, ds(k, 1)], in1=mod_acc[:, i, ci, :],
                                                 op0=ALU.mult, op1=ALU.add).then_inc(s_macc, 1)

            def mod_finish(L, pr):
                for i in range(2):
                    ch = 2 * pr + i
                    dve.wait_ge(s_mred, (L * 3 + pr) * 2 + i + 1)
                    for ci in range(2):
                        ins = dve.tensor_tensor(mod[:, L, ch, ci, :], pair[2][:, MODP + ci * NK:MODP + (ci + 1) * NK],
                                                v(L, V_BMOD, ch * NK, NK), ALU.add)
                    ins.then_inc(s_mod, 1)
                    if ch % 3 == 1:
                        dve.wait_ge(s_mod, L * N_MOD + ch + 1)
                        for ci in range(2):
                            ins = dve.scalar_tensor_tensor(out=gain[:, L, ch // 3, ci, :], in0=mod[:, L, ch, ci, :],
                                                           scalar=1.0, in1=v(L, (V_N1, V_N2)[ch // 3], 0, NK),
                                                           op0=ALU.add, op1=ALU.mult)
                        ins.then_inc(s_gain, 1)

            def norm(i, L, which):
                dve.wait_ge(s_sd, i + 1)
                dve.reciprocal(rstd[:, :], rstd[:, :]).then_inc(s_rstd, 1)
                dve.wait_ge(s_rstd, i + 1)
                dve.wait_ge(s_gain, 2 * L + which + 1)
                for k in range(NK + 1):
                    if k < NK:
                        for ci, a, b in SEG:
                            if k >= 2:
                                dve.wait_ge(s_h, 2 * (i * NK + k - 2) + 1 + ci)
                            dve.scalar_tensor_tensor(out=norm_t[:, k % 2, a:b], in0=x[:, k, a:b],
                                                     scalar=gain[:, L, which, ci, k:k + 1], in1=rstd[:, a:b],
                                                     op0=ALU.mult, op1=ALU.mult).then_inc(s_nt, 1)
                    if k > 0:
                        for ci, a, b in SEG:
                            dve.wait_ge(s_hhi, 2 * (i * NK + k - 1) + 1 + ci)
                            dve.scalar_tensor_tensor(out=in_lo[:, k - 1, a:b], in0=norm_t[:, (k - 1) % 2, a:b],
                                                     scalar=mod[:, L, 3 * which, ci, k - 1:k],
                                                     in1=in_hi[:, k - 1, a:b].bitcast(F32),
                                                     op0=ALU.add, op1=ALU.subtract).then_inc(s_h, 1)

            def residual(N, s, L, ch, m):
                dve.wait_ge(s_lin, N + 1)
                for ci, a, b in SEG:
                    ins = dve.scalar_tensor_tensor(out=x[:, m, a:b], in0=lin[s][:, a:b],
                                                   scalar=mod[:, L, ch, ci, m:m + 1], in1=x[:, m, a:b],
                                                   op0=ALU.mult, op1=ALU.add)
                ins.then_inc(s_xupd, 1)

            dve.wait_ge(s_cond, 1)
            for n in range(2):
                lo(n, n, NK)
            for k in range(NK):
                for i in range(2):
                    mod_unit(0, 0, k, i)
            mod_finish(0, 0)
            for L in range(DEPTH):
                norm(2 * L, L, 0)
                for n in range(N_IN):
                    N = tile_in(L) + n
                    dve.wait_ge(s_lin, N + 1)
                    if n == IN_K or IN_Q <= n < IN_U:
                        e = 0 if n == IN_K else n - IN_Q + 1
                        E = L * (1 + NQ) + e
                        dve.wait_ge(s_qsq, E + 1)
                        if e >= 2:
                            dve.wait_ge(s_qn, 2 * (E - 1))
                        ins = dve.tensor_copy(qk_raw[:, e % 2, :], lin[n % 2])
                        ins.then_inc(s_free, 1)
                    elif n == IN_V:
                        dve.tensor_copy(v_feat[:, :], lin[n % 2]).then_inc(s_free, 1)
                    else:
                        g = n - IN_U
                        if g == 0:
                            dve.wait_ge(s_upad, 3 * (L + 1))
                        dve.tensor_copy(u[:, g, U_P:U_P + TP], lin[n % 2][:, 0:TP]).then_inc(s_u, 1)
                        dve.tensor_copy(u[:, g, U_S:U_S + TS], lin[n % 2][:, TP:T]).then_inc(s_u, 1)
                    lo(N + 2, n % 2, NK)
                    e = 0 if n - 1 == IN_K else n - IN_Q if IN_Q <= n - 1 < IN_U else None
                    if e is not None:
                        E = L * (1 + NQ) + e
                        dve.wait_ge(s_qsd, E + 1)
                        dve.reciprocal(qk_rstd[:, e % 2, :], qk_rstd[:, e % 2, :]).then_inc(s_qrs, 1)
                        dve.wait_ge(s_qrs, E + 1)
                        gn = v(L, V_KG if e == 0 else V_QG, 0)
                        dst = (keys[:, 0:TP], keys[:, TP + PAST:]) if e == 0 else (q[:, e - 1, 0:TP], q[:, e - 1, TP:T])
                        dve.wait_ge(s_free, L * IN_U + n)
                        for (ci, a, b), d in zip(SEG, dst):
                            dve.scalar_tensor_tensor(out=d, in0=qk_raw[:, e % 2, a:b], scalar=gn,
                                                     in1=qk_rstd[:, e % 2, a:b], op0=ALU.mult,
                                                     op1=ALU.mult).then_inc(s_qn, 1)
                        dve.wait_ge(s_qn, 2 * E + 2)
                        if E > 0:
                            dve.wait_ge(s_rp, 2 * E)
                        dve.stream_shuffle(rope[:, 0, :], dst[1], [(i + 16) % 32 for i in range(32)]).then_inc(s_shuf, 1)
                    if n < NK:
                        for i in range(2):
                            mod_unit(L, 1, n, i)
                mod_finish(L, 1)
                for i in range(NU + 1):
                    if i < NU:
                        un = L * NU + i
                        nkeys = P if UNITS[i][0] == 0 else T
                        dve.wait_ge(s_s, un + 1)
                        dve.tensor_reduce(small[:, i % 2, 3:4], lin[i % 2][:, 0:nkeys], AX_X, ALU.max).then_inc(s_max, 1)
                        dve.wait_ge(s_max, un + 1)
                        if i >= 2:
                            dve.wait_ge(s_exp, un - 1)
                        dve.tensor_scalar(small[:, i % 2, 0:1], small[:, i % 2, 3:4], -SCALE, None,
                                          ALU.mult).then_inc(s_neg, 1)
                    if i > 0:
                        un = L * NU + i - 1
                        nkeys = P if UNITS[i - 1][0] == 0 else T
                        dve.wait_ge(s_exp, un + 1)
                        dve.reciprocal(small[:, (i - 1) % 2, 2:3], small[:, (i - 1) % 2, 1:2]).then_inc(s_rec, 1)
                        dve.wait_ge(s_rec, un + 1)
                        dve.tensor_scalar(prob[:, (i - 1) % 2, 0:nkeys], prob[:, (i - 1) % 2, 0:nkeys],
                                          small[:, (i - 1) % 2, 2:3], None, ALU.mult).then_inc(s_prob, 1)
                    if i >= 3 and (i - 2) % NH == 0:
                        o_low(L, (i - 2) // NH - 1)
                    if 4 <= i < 4 + 4 * NK and i % 2 == 0:
                        n = (i - 4) // 2
                        mod_unit(L, 2, n // 2, n % 2)
                    if i in (9, 15, 21, 27):
                        g = (i - 9) // 6
                        dve.wait_ge(s_tree, 4 * (L * NPOOL + g + 1))
                        for at, n in ((U_P, TP), (U_S, TS)):
                            ins = dve.scalar_tensor_tensor(out=u[:, g, at:at + n], in0=tree[:, g % 2, at:at + n],
                                                           scalar=1.0 / WINDOWS[g], in1=u[:, g, at:at + n],
                                                           op0=ALU.mult, op1=ALU.subtract)
                        ins.then_inc(s_pooled, 1)
                o_low(L, NT - 1)
                for g in range(NPOOL):
                    dve.wait_ge(s_phi, L * NPOOL + g + 1)
                    dve.scalar_tensor_tensor(out=in_lo[:, NQ + g, :], in0=lin[g % 2], scalar=v(L, V_PS, g),
                                             in1=in_hi[:, NQ + g, :].bitcast(F32), op0=ALU.mult,
                                             op1=ALU.subtract).then_inc(s_plo, 1)
                for m in range(N_OUT):
                    N = tile_out(L) + m
                    if m == 2:
                        mod_finish(L, 2)
                    if m == 0:
                        dve.wait_ge(s_mod, L * N_MOD + 3)
                    residual(N, m % 2, L, 2, m)
                    lo(N + 2, m % 2, NK)
                norm(2 * L + 1, L, 1)
                for g in range(NG):
                    base = tile_up(L, g)

                    def up_iter(j, nxt, nk, mods, L=L, g=g, base=base):
                        n = (L * NG + g) * FG + j
                        for s in range(2):
                            dve.wait_ge(s_ctr, 2 * n + s + 1)
                            tap = 4 * (2 * n + s)
                            for r, (t, sh) in enumerate(((0, -1), (2, 1))):
                                for ci, a, b in SEG:
                                    d0, d1 = (a + 1, b) if sh < 0 else (a, b - 1)
                                    if r == 1:
                                        dve.wait_ge(s_tap, tap + ci + 1)
                                    ins = dve.scalar_tensor_tensor(
                                        out=conv[:, s, d0:d1], in0=lin[s][:, d0 + sh:d1 + sh],
                                        scalar=v(L, V_TAP[t], s * NF + g * FG + j), in1=conv[:, s, d0:d1],
                                        op0=ALU.mult, op1=ALU.add).then_inc(s_tap, 1)
                            if isinstance(nxt, int):
                                lo(nxt + s, s, nk)
                            else:
                                lo(2 * j + (base + 2 + s), s, nk)
                            if mods:
                                mod_unit(L + 1, 0, j, s)
                    mods = g == 0 and L + 1 < DEPTH
                    up_iter(0, base + 2, NK, mods)
                    if mods:
                        with dve.Fori(1, NK) as j:
                            up_iter(j, None, NK, True)
                        with dve.Fori(NK, FG - 1) as j:
                            up_iter(j, None, NK, False)
                    else:
                        with dve.Fori(1, FG - 1) as j:
                            up_iter(j, None, NK, False)
                    up_iter(FG - 1, base + 2 * FG, FG, False)
                    down = tile_down(L, g)
                    dve.wait_ge(s_mod, (L + 1) * N_MOD)
                    for m in range(NK):
                        if mods and m == 0:
                            mod_finish(L + 1, 0)
                        residual(down + m, m % 2, L, 5, m)
                        if down + m + 2 < DEPTH * PER_LAYER:
                            lo(down + m + 2, m % 2, FG if m + 2 < NK else NK)
            i = 2 * DEPTH
            dve.wait_ge(s_sd, i + 1)
            dve.reciprocal(rstd[:, :], rstd[:, :]).then_inc(s_rstd, 1)
            dve.wait_ge(s_rstd, i + 1)
            for k in range(NK):
                dve.scalar_tensor_tensor(out=yf[:, k, :], in0=x[:, k, :], scalar=v(0, V_FIN, k), in1=rstd[:, :],
                                         op0=ALU.mult, op1=ALU.mult).then_inc(s_y, 1)

        @block.tensor
        def _(pe):
            def split_matmul(dst, s, k, rhs_hi, rhs_lo, kk, first, last):
                passes = ((w_hi, rhs_hi), (w_hi, rhs_lo), (w_lo, rhs_hi))
                for r, (w, rhs) in enumerate(passes):
                    for hf in range(2):
                        a = hf * HALF_T
                        ins = pe.matmul(dst[:, a:a + HALF_T], w[:, s, k, :], rhs[:, kk, a:a + HALF_T],
                                        start=first and r == 0, stop=last and r == 2)
                return ins

            def linear(n, s, nk, rhs_hi, rhs_lo, wait_k=None):
                pe.wait_ge(s_wlo, n + 1)
                for k in range(nk):
                    if wait_k is not None:
                        wait_k(k)
                    ins = split_matmul(lin[s], s, k, rhs_hi, rhs_lo, k, k == 0, k == nk - 1)
                ins.then_inc(s_lin, 1)

            def stat(i):
                pe.wait_ge(s_ss, (i + 1) * NK)
                if i > 0 and i < 2 * DEPTH and i % 2 == 1:
                    pe.wait_ge(s_olo, (i // 2 + 1) * NT)
                for hf in range(2):
                    a = hf * HALF_T
                    ins = pe.matmul(lin[3][:, a:a + HALF_T], ones, ssum[:, a:a + HALF_T], start=True, stop=True)
                ins.then_inc(s_stat, 1)

            def mod_reduce(L, pr):
                for i in range(2):
                    pe.wait_ge(s_macc, (mod_slot(L, pr, NK)) * 4 - 2 + 2 * i)
                    if (L * 3 + pr) * 2 + i > 0:
                        pe.wait_ge(s_mod, (L * 3 + pr) * 2 + i)
                    for r in range(n_red):
                        ins = pe.matmul(pair[2][:, MODP + r:MODP + r + P], mod_acc[:, i, r // NK, (r % NK) * P:(r % NK + 1) * P],
                                        ones, start=True, stop=True)
                    ins.then_inc(s_mred, 1)

            def h_wait(i):
                return lambda k: pe.wait_ge(s_h, 2 * (i * NK + k + 1))

            pe.wait_ge(s_const, 16)
            pe.wait_ge(s_rows, 16 * (5 + 4 + 3 + 3 * DEPTH))
            for L in range(DEPTH):
                if L > 0:
                    pe.wait_ge(s_vec, L)
                for t in range(3):
                    ins = pe.transpose(pair[2][:, t * P:t * P + N_ROWS[t]], rows[0:N_ROWS[t], L, t, :],
                                       ident[0:N_ROWS[t], 0:N_ROWS[t]])
                ins.then_inc(s_vec_t, 1)
            pe.wait_ge(s_x, 32)
            for k in range(NK):
                if k >= 2:
                    pe.wait_ge(s_xe, k - 1)
                for b in range(NT):
                    ins = pe.transpose(pair[k % 2][:, b * P:(b + 1) * P], xin[:, b, k * P:(k + 1) * P], ident)
                ins.then_inc(s_xt, 1)
            stat(0)
            pe.wait_ge(s_vec, DEPTH)
            mod_reduce(0, 0)
            pe.wait_ge(s_xe, NK)

            def q_stat(E):
                pe.wait_ge(s_qsq, E + 1)
                if E % (1 + NQ) > 0:
                    pe.wait_ge(s_qsd, E)
                for hf in range(2):
                    a = hf * HALF_T
                    ins = pe.matmul(lin[3][:, a:a + HALF_T], head_ones, sq[:, E % 2, a:a + HALF_T], start=True, stop=True)
                ins.then_inc(s_qst, 1)

            for L in range(DEPTH):
                for n in range(N_IN):
                    N = tile_in(L) + n
                    if n >= IN_U + 2:
                        pe.wait_ge(s_u, 2 * (L * NPOOL + n - IN_U - 1))
                    elif n >= 2:
                        pe.wait_ge(s_free, L * IN_U + n - 1)
                    elif L > 0:
                        pe.wait_ge(s_xupd, upd_down(L - 1, NG - 1) + NK - 1 + n)
                    linear(N, n % 2, NK, in_hi, in_lo, h_wait(2 * L) if n == 0 else None)
                    if n == IN_K + 1:
                        pe.wait_ge(s_sd, 2 * L + 1)
                        q_stat(L * (1 + NQ))
                    if IN_Q < n <= IN_U:
                        q_stat(L * (1 + NQ) + n - IN_Q)
                    if n == IN_Q:
                        pe.wait_ge(s_free, L * IN_U + IN_V + 1)
                        pe.wait_ge(s_past, 32 * (L + 1))
                        for b in range(NT):
                            pe.transpose(pair[2][:, b * P:(b + 1) * P], v_feat[:, b * P:(b + 1) * P], ident)
                        pe.transpose(pair[2][:, T:T + P], past[:, 0, :], ident).then_inc(s_vt, 1)
                    if n == IN_Q + 2:
                        pe.wait_ge(s_pk, L + 1)
                        pe.wait_ge(s_qn, 2 * L * (1 + NQ) + 1)
                        pe.transpose(pair[2][:, T:T + P], keys[:, 0:P], ident).then_inc(s_kt, 1)
                mod_reduce(L, 1)

                def scores(i):
                    b, h = UNITS[i]
                    un = L * NU + i
                    a = (h % 2) * HALF
                    kk = keys if h // GRP == h % 2 else keys_x
                    if i < 2:
                        pe.wait_ge(s_u, 2 * (L * NPOOL + NPOOL - 1 + i))
                        if i == 0:
                            pe.wait_ge(s_kx, 2 * (L + 1))
                    else:
                        pe.wait_ge(s_exp, un - 1)
                    pe.wait_ge(s_qk, L * (1 + NQ) + 2 + h // 2)
                    qs = q[a:a + HALF, h // 2, b * P:(b + 1) * P]
                    if b == 0:
                        ins = pe.matmul(lin[i % 2][:, 0:P], qs, kk[a:a + HALF, 0:P], start=True, stop=True)
                    else:
                        for hf in range(2):
                            c0 = hf * HALF_T
                            ins = pe.matmul(lin[i % 2][:, c0:c0 + HALF_T], qs, kk[a:a + HALF, TP + c0:TP + c0 + HALF_T],
                                            start=True, stop=True)
                    ins.then_inc(s_s, 1)

                def transpose_prob(i):
                    un = L * NU + i
                    pe.wait_ge(s_prob, un + 1)
                    if i > 0:
                        pe.wait_ge(s_pte, un)
                    elif True:
                        pe.wait_ge(s_val, L + 1)
                        pe.wait_ge(s_kout, L + 1)
                    for kt in range(1 if UNITS[i][0] == 0 else NT):
                        ins = pe.transpose(pair[2][:, kt * P:(kt + 1) * P], prob[:, i % 2, kt * P:(kt + 1) * P], ident)
                    ins.then_inc(s_pt, 1)

                def weigh(i):
                    b, h = UNITS[i]
                    un = L * NU + i
                    a = (h % 2) * HALF
                    g = h // GRP
                    pe.wait_ge(s_pte, un + 1)
                    if h == 0:
                        if b >= 2:
                            pe.wait_ge(s_olo, L * NT + b - 1)
                        if b == 0:
                            pe.wait_ge(s_qsd, (L + 1) * (1 + NQ))
                    dst = pair[3][a:a + HALF, (b % 2) * 512 + h // 2 * P:(b % 2) * 512 + (h // 2 + 1) * P]
                    nkt = 1 if b == 0 else NT
                    for kt in range(nkt):
                        vv = val[:, 0, g * HD:(g + 1) * HD] if b == 0 else \
                            past[:, 1, g * HD:(g + 1) * HD] if kt == 0 else val[:, kt, g * HD:(g + 1) * HD]
                        ins = pe.matmul(dst, vv, prob_t[:, i % 2, kt * P:(kt + 1) * P], start=kt == 0, stop=kt == nkt - 1)
                    ins.then_inc(s_o, 1)

                scores(0)
                scores(1)
                for i in range(NU):
                    if i + 2 < NU:
                        scores(i + 2)
                    if i > 0:
                        weigh(i - 1)
                    transpose_prob(i)
                weigh(NU - 1)
                pe.wait_ge(s_wp, 16 * (L + 1))
                for g in range(NPOOL):
                    pe.wait_ge(s_pooled, L * NPOOL + g + 1)
                    if g < 2:
                        pe.wait_ge(s_exp, (L + 1) * NU - 1 + g)
                    else:
                        pe.wait_ge(s_plo, L * NPOOL + g - 1)
                    d = lin[g % 2]
                    pe.matmul(d[:, 0:TP], wp[:, g, :], u[:, g, U_P:U_P + TP], start=True, stop=True)
                    cut = HALF_T - TP
                    pe.matmul(d[:, TP:HALF_T], wp[:, g, :], u[:, g, U_S:U_S + cut], start=True, stop=True)
                    pe.matmul(d[:, HALF_T:T], wp[:, g, :], u[:, g, U_S + cut:U_S + TS], start=True,
                              stop=True).then_inc(s_pm, 1)
                for m in range(N_OUT):
                    N = tile_out(L) + m
                    if m < 2:
                        pe.wait_ge(s_plo, L * NPOOL + NPOOL - 1 + m)
                        pe.wait_ge(s_olo, (L + 1) * NT)
                    else:
                        pe.wait_ge(s_xupd, upd_out(L) + m - 1)
                    linear(N, m % 2, NK, in_hi, in_lo,
                           (lambda k: pe.wait_ge(s_plo, (L + 1) * NPOOL) if k == NK - 1 else None) if m == 0 else None)
                    if m == 1:
                        mod_reduce(L, 2)
                stat(2 * L + 1)
                for g in range(NG):
                    base = tile_up(L, g)
                    def up_iter(j, first, L=L, g=g, base=base):
                        for s in range(2):
                            if first:
                                if g == 0:
                                    pe.wait_ge(s_xupd, upd_out(L) + NK - 1 + s)
                                else:
                                    pe.wait_ge(s_xupd, upd_down(L, g - 1) + NK - 1 + s)
                            else:
                                pe.wait_ge(s_tap, 8 * j + (8 * (L * NG + g) * FG - 4 + 4 * s))
                            linear(2 * j + (base + s), s, NK, in_hi, in_lo,
                                   h_wait(2 * L + 1) if first and g == 0 and s == 0 else None)
                    up_iter(0, True)
                    with pe.Fori(1, FG) as j:
                        up_iter(j, False)
                    if g == 0 and L + 1 < DEPTH:
                        mod_reduce(L + 1, 0)
                    down = tile_down(L, g)
                    done = (L * NG + g) * FG

                    def down_iter(i, first):
                        for s in range(2):
                            if first:
                                pe.wait_ge(s_tap, 8 * (done + FG) - 4 + 4 * s)
                            else:
                                pe.wait_ge(s_xupd, upd_down(L, g) + 2 * i + (s - 1))
                            linear(2 * i + (down + s), s, FG, act_hi, act_lo,
                                   (lambda k: pe.wait_ge(s_alo, done + k + 1)) if first and s == 0 else None)
                    down_iter(0, True)
                    with pe.Fori(1, NK // 2) as i:
                        down_iter(i, False)
                stat(2 * L + 2)
            for b in range(NT):
                for hf in range(2):
                    i = 2 * b + hf
                    if i >= 8:
                        pe.wait_ge(s_ye, i - 7)
                    for kk in range(4):
                        k = 4 * hf + kk
                        if b == 0:
                            pe.wait_ge(s_y, k + 1)
                        if i in (6, 7):
                            pe.wait_ge(s_sd, 2 * DEPTH + 1)
                        ins = pe.transpose(y_bank(i)[:, kk * P:(kk + 1) * P], yf[:, k, b * P:(b + 1) * P], ident)
                    ins.then_inc(s_yt, 1)


_INS = ['x_prompt', 'x_sample', 'cache_k', 'cache_v', 'c', 'c_ctx', 'w_mod', 'b_mod', 'norm1_g', 'w_in', 'q_norm_g',
        'k_norm_g', 'w_pool', 'pool_scale', 'w_out', 'norm2_g', 'w_up', 'conv_w', 'conv_b', 'w_down', 'final_norm_g']


def kernel(**inputs):
    import numpy as _np
    import concourse.bacc as _bacc
    from concourse import mybir as _mybir
    from concourse.bass_utils import run_bass_kernel_spmd as _run

    nc = _bacc.Bacc("TRN2", target_bir_lowering=False, num_devices=1)
    arrays, args = {}, []
    for name in _INS:
        arrays[f"in_{name}_dram"] = _np.ascontiguousarray(inputs[name])
    b, s, d = inputs['x_prompt'].shape
    db, ds_, _ = inputs['x_sample'].shape
    depth = inputs['w_in'].shape[0]
    kvh, hd = inputs['cache_k'].shape[3:]
    arrays["in_consts_dram"] = shape_constants(s, ds_, hd)
    for name, a in arrays.items():
        args.append(nc.dram_tensor(name, a.shape, _mybir.dt.from_np(a.dtype), kind="ExternalInput").ap())
    outs = [(b, s, d), (db, ds_, d), (b, depth, s, kvh, hd), (b, depth, s, kvh, hd)]
    for i, shape in enumerate(outs):
        args.append(nc.dram_tensor(f"out_{i}_dram", shape, _mybir.dt.float32, kind="ExternalOutput").ap())
    build(nc, *args)
    r = _run(nc, [arrays], core_ids=[0])
    return tuple(r.results[0][f"out_{i}_dram"] for i in range(len(outs)))
```

```python
from contextlib import ExitStack

import numpy as np

import concourse.bass as bass
from concourse import mybir

F32 = mybir.dt.float32
F32R = mybir.dt.float32r
ALU = mybir.AluOpType
ACT = mybir.ActivationFunctionType
AX_X = mybir.AxisListType.X

P = 128
HALF = P // 2
EPS = 1e-6
GRID_W = 64
ROPE_THETA = 10000.0
WINDOWS = (2, 4, 8, 16)
PAD = max(WINDOWS) // 2


def ds(start, size):
    return bass.ds(start, size)


def shape_constants(n_prompt, n_sample, head_dim):
    ident = np.eye(P, dtype=np.float32)
    block = np.kron(np.eye(P // head_dim), np.ones((head_dim, head_dim))).astype(np.float32)
    ones = np.ones((P, P), np.float32)
    quarter = head_dim // 4
    inv = (np.float32(ROPE_THETA) ** (-np.arange(quarter, dtype=np.float32) / np.float32(quarter))).astype(np.float32)
    t = np.arange(n_sample)
    where = np.stack([t // GRID_W, t % GRID_W]).astype(np.float32)
    d = np.arange(P) % head_dim
    axis, second, freq = d // (2 * quarter), (d // quarter) % 2, d % quarter
    angle = (where[axis] * inv[freq][:, None]).astype(np.float32)
    sign = np.where(second == 1, 1.0, -1.0)[:, None]
    edges = np.ones((len(WINDOWS), 2, 2, PAD), np.float32)
    for g, w in enumerate(WINDOWS):
        for s, n in enumerate((n_prompt, n_sample)):
            at = np.concatenate([np.arange(PAD), np.arange(n - PAD, n)])
            count = np.clip(at + w - w // 2, 0, n) - np.clip(at - w // 2, 0, n)
            edges[g, s] = (w / count).reshape(2, PAD)
    return np.concatenate([
        ident, block, ones, np.cos(angle), (np.sin(angle) * sign),
        np.broadcast_to(edges.reshape(1, -1), (P, edges.size))], axis=1).astype(np.float32)


def build(nc, x_prompt, x_sample, cache_k, cache_v, c, c_ctx, w_mod, b_mod, norm1_g, w_in,
          q_norm_g, k_norm_g, w_pool, pool_scale, w_out, norm2_g, w_up, conv_w, conv_b,
          w_down, final_norm_g, consts, y_prompt, y_sample, new_k, new_v):
    DEPTH, D, IN_WIDTH = w_in.shape
    TP, TS = x_prompt.shape[1], x_sample.shape[1]
    T = TP + TS
    HALF_T = T // 2
    PAST = cache_k.shape[2]
    HD = cache_k.shape[4]
    KV = cache_k.shape[3] * HD
    NPOOL = w_pool.shape[1]
    AW = D - NPOOL * P
    NH = AW // HD
    GRP = NH // cache_k.shape[3]
    FF = w_down.shape[1]
    NK = D // P
    NT = T // P
    NQ = AW // P
    NF = FF // P
    NG = 2
    FG = NF // NG
    N_MOD = 6
    SCALE = float(HD) ** -0.5
    assert TP == P and TS % P == 0 and KV == P and PAST == P and NF % NG == 0 and HALF_T % 2 == 0
    SEG = ((0, 0, TP), (1, TP, T))

    N_IN, N_OUT = IN_WIDTH // P, NK
    PER_GROUP = 2 * FG + NK
    PER_LAYER = N_IN + N_OUT + NG * PER_GROUP
    IN_U, IN_K, IN_V, IN_Q = 0, NPOOL, NPOOL + 1, NPOOL + 2
    IN_COLUMN = [AW + 2 * KV + P * g for g in range(NPOOL)] + [AW, AW + KV] + [P * t for t in range(NQ)]
    NE = 1 + NQ
    E_TILE = [IN_K] + [IN_Q + t for t in range(NQ)]

    def tile_in(L):
        return L * PER_LAYER

    def tile_out(L):
        return tile_in(L) + N_IN

    def tile_up(L, g):
        return tile_out(L) + N_OUT + g * PER_GROUP

    def tile_down(L, g):
        return tile_up(L, g) + 2 * FG

    BLOCKS = [1, 0] + list(range(2, NT))
    UNITS = [(b, h) for b in BLOCKS for h in range(NH)]
    NU = len(UNITS)

    with ExitStack() as ctx:
        def sb(name, shape, dt=F32, at=ctx):
            return at.enter_context(nc.sbuf_tensor(name, shape, dt))

        def sem(name):
            return ctx.enter_context(nc.semaphore(name))

        x = sb("x", [P, NK, T])
        w_raw = sb("w_raw", [P, 2, FG, P])
        w_hi = sb("w_hi", [P, 2, FG, P], F32R)
        w_lo = sb("w_lo", [P, 2, FG, P], F32R)
        mod_raw = sb("mod_raw", [P, 2, D])
        mod_acc = sb("mod_acc", [P, 2, D])
        n_const = consts.shape[1]
        cst = sb("cst", [P, n_const])
        ident, head_ones, ones = (cst[:, i * P:(i + 1) * P] for i in range(3))
        cos, sin = (cst[:, 3 * P + i * TS:3 * P + (i + 1) * TS] for i in range(2))
        edge = cst[:, 3 * P + 2 * TS:n_const].rearrange("p (g s e c) -> p g s e c", g=NPOOL, s=2, e=2)
        vec = sb("vec", [P, DEPTH, 3, P])
        mod = sb("mod", [P, DEPTH, N_MOD, 2, NK])
        gain = sb("gain", [P, DEPTH, 2, 2, NK])
        cond = sb("cond", [P, 2, NK])
        eps = sb("eps", [P, 1])
        wp = sb("wp", [P, NPOOL, P])
        past = sb("past", [P, 2, P])
        val = sb("val", [P, NT, P])
        k_out = sb("k_out", [P, P])
        sq = sb("sq", [P, 2, T])
        prob = sq
        ssum = sb("ssum", [P, T])
        rstd = sb("rstd", [P, T])
        v_feat = rstd
        small = sb("small", [P, 2, 4])
        rtok = sb("rtok", [P, NT])

        with ExitStack() as inputs:
            in_hi = sb("in_hi", [P, NK, T], F32R, at=inputs)
            in_lo = sb("in_lo", [P, NK, T], F32R, at=inputs)
            with ExitStack() as own:
                xin = sb("xin", [P, NT, D], at=own)
                rows = sb("rows", [P, DEPTH, 3, P], at=own)
                cond_rows = sb("cond_rows", [2 * NK, P], at=own)
                N_FIRST = 6
                w_first = sb("w_first", [P, N_FIRST, 2 * D], at=own)
            with ExitStack() as own:
                norm_t = sb("norm_t", [P, 2, T], at=own)
            with ExitStack() as own:
                qk = sb("qk", [P, 3, T], at=own)
                qk_rstd = sb("qk_rstd", [P, 2, T], at=own)
                keys = sb("keys", [P, T + PAST], at=own)
                q_st = sb("q_st", [P, NH, T], F32R, at=own)
                k_hi = sb("k_hi", [P, KV // HD, T + PAST], F32R, at=own)
                k_lo = sb("k_lo", [P, KV // HD, T + PAST], F32R, at=own)
                rope = sb("rope", [P, 2, TS], at=own)
                prob_t = sb("prob_t", [P, 2, T], at=own)
                U_P, U_S = PAD, TP + 2 * PAD
                U_W = U_S + TS + PAD
                u = sb("u", [P, NPOOL, U_W], at=own)
                tree = sb("tree", [P, 2, U_W], at=own)
            with ExitStack() as own:
                conv = sb("conv", [P, 2, T], at=own)
                act_hi = sb("act_hi", [P, FG, T], F32R, at=own)
                act_lo = sb("act_lo", [P, FG, T], F32R, at=own)
                silu_a = sb("silu_a", [P, T], at=own)
        with ExitStack() as own:
            yout = sb("yout", [P, NT, D], at=own)
            yf = sb("yf", [P, 2, T], at=own)

        pair = [ctx.enter_context(nc.psum_tensor(f"pair{i}", [P, 2 * 512], F32)) for i in range(4)]
        LIN0 = 512 - HALF_T
        lin = [pair[i][:, LIN0:LIN0 + T] for i in range(4)]
        MODP = 832

        V_BMOD, V_CONVB, V_N1, V_N2, V_PS, V_QG, V_KG = (0, 0), (0, 48), (0, 92), (0, 100), (0, 108), (0, 112), (0, 113)
        V_TAP = ((1, 0), (1, NF * 2), (2, 0))
        V_FIN = (2, 44)
        N_ROWS = (114, 88, 52)
        assert 2 * NF == 44 and NK == 8

        def v(L, place, i, n=1):
            return vec[:, L, place[0], ds(place[1] + i, n)]

        s_const, s_rows, s_x = sem("const_loaded"), sem("rows_loaded"), sem("x_loaded")
        s_crow = sem("cond_rows_loaded")
        s_vec_t, s_vec = sem("vec_transposed"), sem("vec_ready")
        s_cond, s_eps = sem("cond_ready"), sem("eps_ready")
        s_xt, s_xe = sem("x_transposed"), sem("x_evacuated")
        s_raw = [sem(f"w_loaded{i}") for i in range(2)]
        s_whi, s_wlo = sem("w_hi_ready"), sem("w_lo_ready")
        s_lin, s_free = sem("lin_done"), sem("lin_free")
        s_gain, s_mfirst = sem("gain_ready"), sem("first_used")
        s_mraw = [sem(f"mod_loaded{i}") for i in range(2)]
        s_macc, s_mred, s_mod = sem("mod_accumulated"), sem("mod_reduced"), sem("mod_ready")
        s_xupd, s_sq, s_ss, s_ss0 = sem("x_updated"), sem("squares_ready"), sem("squares_summed"), sem("sum_cleared")
        s_stat, s_sd, s_rstd = sem("stat_done"), sem("std_ready"), sem("rstd_ready")
        s_nt, s_hhi, s_h = sem("normed"), sem("h_hi_ready"), sem("h_ready")
        s_qsq, s_qst, s_qsd, s_qrs = sem("qk_squared"), sem("qk_stat"), sem("qk_std"), sem("qk_rstd_ready")
        s_qraw, s_qn, s_shuf = sem("qk_copied"), sem("qk_normed"), sem("qk_shuffled")
        s_rp, s_qk = sem("rope_part"), sem("qk_ready")
        s_vf, s_vt, s_val, s_pkt, s_pk = sem("v_copied"), sem("v_transposed"), sem("values_ready"), sem("past_transposed"), sem("past_key_ready")
        s_kt, s_kout = sem("new_key_transposed"), sem("new_key_copied")
        s_past, s_wp = sem("past_loaded"), sem("w_pool_loaded")
        s_out = sem("outputs_written")
        s_upad, s_u, s_tree, s_tstep, s_pooled = sem("pads_cleared"), sem("u_ready"), sem("window_sums"), sem("tree_step"), sem("pooled")
        s_pm, s_phi, s_plo = sem("pool_mixed"), sem("pool_hi"), sem("pool_lo")
        s_qs_hi, s_qs, s_ks_hi, s_ks = sem("query_hi"), sem("query_split"), sem("key_hi"), sem("keys_split")
        s_first, s_const0 = [sem(f"first_loaded{i}") for i in range(8)], sem("ident_loaded")
        s_s, s_max, s_neg, s_exp, s_rec, s_prob = sem("scores_done"), sem("max_ready"), sem("neg_max_ready"), sem("exp_done"), sem("reciprocal_ready"), sem("prob_ready")
        s_pt, s_pte, s_o, s_ohi, s_olo = sem("prob_transposed"), sem("prob_t_ready"), sem("head_done"), sem("o_hi"), sem("o_lo")
        s_ctr, s_tap, s_silu = sem("conv_centre"), sem("conv_tap"), sem("silu_ready")
        s_act, s_ahi, s_alo = sem("act_ready"), sem("act_hi_ready"), sem("act_lo_ready")
        s_y, s_yt, s_ye, s_yn = sem("y_gained"), sem("y_transposed"), sem("y_copied"), sem("y_normed")

        block = ctx.enter_context(nc.Block())

        w_in_v = [w_in[L].rearrange("(k p) n -> p k n", p=P) for L in range(DEPTH)]
        w_out_v = [w_out[L].rearrange("(k p) n -> p k n", p=P) for L in range(DEPTH)]
        w_up_v = [w_up[L].rearrange("(k p) n -> p k n", p=P) for L in range(DEPTH)]
        w_down_v = [w_down[L].rearrange("(k p) n -> p k n", p=P) for L in range(DEPTH)]

        def unit(C, k):
            return (C - 2) * NK + k

        def mlp_chunks(L, g):
            first = L * N_MOD + 5 + 3 * g
            return [C if C < DEPTH * N_MOD else None for C in range(first, first + 3)]

        def o_bank(pos):
            return pair[3][:, (pos % 2) * 512:(pos % 2) * 512 + NQ * P].rearrange("p (t c) -> p t c", t=NQ)

        def e_of(n):
            return E_TILE.index(n) if n in E_TILE else None

        def upd_out(L):
            return L * (1 + NG) * NK

        def upd_down(L, g):
            return upd_out(L) + (1 + g) * NK

        
        @block.sync
        def _(sp):
            def load_w(n, s, src, nk):
                if not isinstance(n, int) or n >= 2:
                    sp.wait_ge(s_wlo, n - 1)
                sp.dma_start(w_raw[:, s, 0:nk, :], src).then_inc(s_raw[s], 16)

            def load_mod(C, k, s):
                if C is None:
                    return
                if not isinstance(k, int) or unit(C, k) >= 2:
                    sp.wait_ge(s_macc, 2 * k + (2 * unit(C, 0) - 2))
                L, ch = C // N_MOD, C % N_MOD
                sp.dma_start(mod_raw[:, s, :], w_mod[L, ds(k * P, P), ch * D:(ch + 1) * D]).then_inc(s_mraw[s], 16)

            def load_first(k):
                if k >= N_FIRST:
                    sp.wait_ge(s_mfirst, k - N_FIRST + 1)
                sp.dma_start(w_first[:, k % N_FIRST, :], w_mod[0, k * P:(k + 1) * P, 0:2 * D]).then_inc(s_first[k], 16)

            def load_in(L, n):
                load_w(tile_in(L) + n, n % 2, w_in_v[L][:, :, IN_COLUMN[n]:IN_COLUMN[n] + P], NK)

            def load_out(L, m):
                load_w(tile_out(L) + m, m % 2, w_out_v[L][:, :, m * P:(m + 1) * P], NK)

            sp.dma_start(ident, consts[:, 0:P]).then_inc(s_const0, 16)
            for i, src in enumerate((c_ctx, c.rearrange("a d -> (a d)"))):
                sp.dma_start(cond_rows[i * NK:(i + 1) * NK, :], src.rearrange("(r c) -> r c", c=P)).then_inc(s_crow, 16)
            for src, at, n, t in ((b_mod, 0, 48, 0), (conv_b, 48, 44, 0), (norm1_g, 92, NK, 0), (norm2_g, 100, NK, 0),
                                  (pool_scale, 108, NPOOL, 0)):
                sp.dma_start(rows[at:at + n, :, t, :], src.rearrange("l (r c) -> r l c", c=P)).then_inc(s_rows, 16)
            for src, at in ((q_norm_g, 112), (k_norm_g, 113)):
                for i in range(2):
                    sp.dma_start(rows[at:at + 1, :, 0, i * HD:(i + 1) * HD],
                                 src.rearrange("l (r c) -> r l c", r=1)).then_inc(s_rows, 16)
            for tap, (t, at) in enumerate(V_TAP):
                sp.dma_start(rows[at:at + 2 * NF, :, t, :],
                             conv_w[:, tap, :].rearrange("l (r c) -> r l c", c=P)).then_inc(s_rows, 16)
            for L in range(DEPTH):
                sp.dma_start(rows[44:44 + NK, L, 2, :], final_norm_g.rearrange("(r c) -> r c", c=P)).then_inc(s_rows, 16)
            for k in range(4):
                load_first(k)
            sp.dma_start(xin[:, 0, :], x_prompt[0]).then_inc(s_x, 16)
            sp.dma_start(xin[:, 1:NT, :], x_sample[0].rearrange("(t p) d -> p t d", p=P)).then_inc(s_x, 16)
            sp.dma_start(cst[:, P:n_const], consts[:, P:n_const]).then_inc(s_const, 16)
            for k in range(4, NK):
                load_first(k)
            for n in range(4):
                load_in(0, n)
            for s in range(2):
                load_mod(2, s, s)
            for L in range(DEPTH):
                if L > 0:
                    sp.wait_ge(s_o, L * NU)
                sp.dma_start(past[:, 0, :], cache_k[0, L].rearrange("t h d -> t (h d)")).then_inc(s_past, 16)
                sp.dma_start(past[:, 1, :], cache_v[0, L].rearrange("t h d -> t (h d)")).then_inc(s_past, 16)
                sp.dma_start(wp[:, :, :], w_pool[L].rearrange("g c d -> c g d")).then_inc(s_wp, 16)
                units_at = {0: (2, 3), 1: (4, 5), 2: (6,), 3: (7,)} if L == 0 else {}
                for n in range(N_IN):
                    if n + 4 < N_IN:
                        load_in(L, n + 4)
                    else:
                        load_out(L, n + 4 - N_IN)
                    for k in units_at.get(n, ()):
                        load_mod(2, k, k % 2)
                    if L == 0 and n in (4, 5):
                        load_mod(3, n - 4, n - 4)
                if L == 0:
                    for k in range(2, NK):
                        load_mod(3, k, k % 2)
                    for s in range(2):
                        load_mod(4, s, s)

                def load_up(j, L=L, g=0):
                    for s in range(2):
                        load_w(tile_up(L, g) + 2 * j + s, s,
                               w_up_v[L][:, :, ds(s * FF + (g * FG + j) * P, P)], NK)

                def load_down(i, L, g):
                    for s in range(2):
                        load_w(tile_down(L, g) + 2 * i + s, s,
                               w_down_v[L][:, g * FG:(g + 1) * FG, ds((2 * i + s) * P, P)], FG)

                for m in range(4):
                    load_out(L, 4 + m)
                    if L == 0 and m > 0:
                        for s in range(2):
                            load_mod(4, 2 * m + s, s)
                load_up(0, L, 0)
                for s in range(2):
                    load_mod(L * N_MOD + 5, s, s)
                load_up(1, L, 0)
                for g in range(NG):
                    A, B, C = mlp_chunks(L, g)
                    with sp.Fori(2, 5) as j:
                        load_up(j, L, g)
                        for s in range(2):
                            load_mod(A, 2 * j + (s - 2), s)
                    load_up(5, L, g)
                    for s in range(2):
                        load_mod(B, s, s)
                    with sp.Fori(6, 8) as j:
                        load_up(j, L, g)
                    with sp.Fori(8, FG) as j:
                        load_up(j, L, g)
                        for s in range(2):
                            load_mod(B, 2 * j + (s - 14), s)
                    load_down(0, L, g)
                    for s in range(2):
                        load_mod(C, s, s)
                    load_down(1, L, g)
                    for m in range(4):
                        load_w(tile_down(L, g) + 4 + m, m % 2,
                               w_down_v[L][:, g * FG:(g + 1) * FG, (4 + m) * P:(5 + m) * P], FG)
                        if m > 0:
                            for s in range(2):
                                load_mod(C, 2 * m + s, s)
                    if g + 1 < NG:
                        load_up(0, L, g + 1)
                        for s in range(2):
                            load_mod(mlp_chunks(L, g + 1)[0], s, s)
                        load_up(1, L, g + 1)
                    elif L + 1 < DEPTH:
                        for n in range(4):
                            load_in(L + 1, n)
            for b in range(NT):
                sp.wait_ge(s_yn, b + 1)
                dst = y_prompt[0] if b == 0 else y_sample[0, (b - 1) * P:b * P, :]
                sp.dma_start(dst, yout[:, b, :]).then_inc(s_out, 16)
            sp.wait_ge(s_out, 16 * (NT + 2 * DEPTH))

        @block.gpsimd
        def _(pool):
            pool.memset(eps[:, :], EPS).then_inc(s_eps, 1)

            def clear_sum(i):
                if i > 0:
                    pool.wait_ge(s_stat, i)
                pool.memset(ssum[:, :], 0.0).then_inc(s_ss0, 1)

            def add_squares(i, base, m):
                if isinstance(m, int) and m == 0:
                    pool.wait_ge(s_ss0, i + 1)
                else:
                    pool.wait_ge(s_ss, base + m)
                pool.wait_ge(s_sq, base + m + 1)
                pool.tensor_tensor(ssum[:, :], ssum[:, :], sq_slot(m), ALU.add).then_inc(s_ss, 1)

            def sq_slot(m):
                return sq[:, m % 2, :]

            clear_sum(0)
            for m in range(NK):
                add_squares(0, 0, m)
            for L in range(DEPTH):
                if L > 0:
                    pool.wait_ge(s_lin, tile_in(L))
                else:
                    pool.wait_ge(s_mfirst, NK)
                    pool.wait_ge(s_xe, NK)
                    pool.wait_ge(s_vec, DEPTH)
                for at in (0, U_P + TP, U_S + TS):
                    pool.memset(u[:, :, at:at + PAD], 0.0).then_inc(s_upad, 1)
                done = L * sum(range(1, NPOOL + 1))
                pool.wait_ge(s_upad, 3 * (L + 1))
                if L == 0:
                    pool.wait_ge(s_const, 16)
                for g in range(NPOOL):
                    pool.wait_ge(s_u, 2 * (L * NPOOL + g + 1))
                    src, lo, hi = u[:, g, :], 0, U_W
                    for r in range(g + 1):
                        left, right = (1, 0) if r == 0 else (2 ** (r - 1), 2 ** (r - 1))
                        lo, hi = lo + left, hi - right
                        dst = tree[:, r % 2, :]
                        if r == 0 and L * NPOOL + g > 0:
                            pool.wait_ge(s_pooled, L * NPOOL + g)
                        if r > 0:
                            pool.wait_ge(s_tstep, done)
                        pool.tensor_tensor(dst[:, lo:hi], src[:, lo - left:hi - left], src[:, lo + right:hi + right],
                                           ALU.add).then_inc(s_tstep, 1)
                        done += 1
                        src = dst
                    pool.wait_ge(s_tstep, done)
                    for s, (at, n) in enumerate(((U_P, TP), (U_S, TS))):
                        for e_, a0 in enumerate((at, at + n - PAD)):
                            pool.tensor_tensor(src[:, a0:a0 + PAD], src[:, a0:a0 + PAD], edge[:, g, s, e_, :],
                                               ALU.mult).then_inc(s_tree, 1)
                for e in range(NE):
                    E = L * NE + e
                    tgt = keys[:, TP + PAST:TP + PAST + TS] if e == 0 else qk[:, e % 3, TP:T]
                    if E > 0:
                        pool.wait_ge(s_qk, E)
                    pool.wait_ge(s_shuf, E + 1)
                    pool.tensor_tensor(rope[:, 1, :], rope[:, 0, :], sin, ALU.mult).then_inc(s_rp, 1)
                    pool.tensor_tensor(tgt, tgt, cos, ALU.mult).then_inc(s_rp, 1)
                    pool.wait_ge(s_rp, 2 * E + 2)
                    pool.tensor_tensor(tgt, tgt, rope[:, 1, :], ALU.add).then_inc(s_qk, 1)
                clear_sum(2 * L + 1)
                base = (2 * L + 1) * NK
                for m in range(NK):
                    add_squares(2 * L + 1, base, m)
                for g in range(NG):
                    def gate(j, L=L, g=g):
                        n = (L * NG + g) * FG + j
                        pool.wait_ge(s_silu, n + 1)
                        pool.wait_ge(s_tap, 8 * n + 8)
                        pool.tensor_tensor(silu_a[:, :], silu_a[:, :], conv[:, 1, :], ALU.mult).then_inc(s_act, 1)
                        pool.wait_ge(s_act, n + 1)
                        pool.tensor_copy(act_hi[:, j, :], silu_a[:, :]).then_inc(s_ahi, 1)
                        pool.wait_ge(s_ahi, n + 1)
                        pool.tensor_tensor(act_lo[:, j, :], silu_a[:, :], act_hi[:, j, :].bitcast(F32),
                                           ALU.subtract).then_inc(s_alo, 1)
                    with pool.Fori(0, FG) as j:
                        gate(j)
                clear_sum(2 * L + 2)
                base = (2 * L + 2) * NK
                for m in range(NK):
                    add_squares(2 * L + 2, base, m)

        @block.scalar
        def _(act_e):
            def hi(n, s, nk):
                act_e.wait_ge(s_raw[s], 16 * slot_loads(n, s))
                if not isinstance(n, int) or n >= 2:
                    act_e.wait_ge(s_lin, n - 1)
                act_e.activation(w_hi[:, s, 0:nk, :], w_raw[:, s, 0:nk, :], ACT.Copy).then_inc(s_whi, 1)

            def slot_loads(n, s):
                return n // 2 + 1 if isinstance(n, int) else (n - s) // 2 + 1

            def hi_at(base, i, s, nk):
                act_e.wait_ge(s_raw[s], 16 * (i + (base // 2 + 1)))
                act_e.wait_ge(s_lin, 2 * i + (base + s - 1))
                act_e.activation(w_hi[:, s, 0:nk, :], w_raw[:, s, 0:nk, :], ACT.Copy).then_inc(s_whi, 1)

            def squares(count, upd, m):
                act_e.wait_ge(s_xupd, upd)
                if not isinstance(count, int) or count >= 2:
                    act_e.wait_ge(s_ss, count - 1)
                act_e.activation(sq[:, m % 2, :], x[:, m, :], ACT.Square).then_inc(s_sq, 1)

            def norm(i, L, which):
                act_e.wait_ge(s_stat, i + 1)
                if i > 0:
                    act_e.wait_ge(s_nt, i * NK * 2)
                act_e.activation(rstd[:, :], lin[3], ACT.Sqrt, bias=eps[:, :], scale=1.0 / D).then_inc(s_sd, 1)
                if L is None:
                    return
                for k in range(NK):
                    for ci, a, b in SEG:
                        act_e.wait_ge(s_nt, 2 * (i * NK + k) + 1 + ci)
                        act_e.activation(in_hi[:, k, a:b], norm_t[:, k % 2, a:b], ACT.Identity,
                                         bias=mod[:, L, 3 * which, ci, k:k + 1]).then_inc(s_hhi, 1)

            act_e.wait_ge(s_vec_t, 1)
            act_e.activation(cond[:, :, :].rearrange("p a b -> p (a b)"), pair[2][0:P, 0:2 * NK], ACT.Silu).then_inc(s_cond, 1)
            for L in range(DEPTH):
                act_e.wait_ge(s_vec_t, L + 2)
                for t in range(3):
                    ins = act_e.activation(vec[:, L, t, 0:N_ROWS[t]], pair[2][:, t * P:t * P + N_ROWS[t]], ACT.Copy)
                ins.then_inc(s_vec, 1)
            for k in range(NK):
                act_e.wait_ge(s_xt, k + 1)
                act_e.activation(x[:, k, :], pair[2 + k % 2][:, 0:T], ACT.Copy).then_inc(s_xe, 1)
                act_e.wait_ge(s_xe, k + 1)
                if k >= 2:
                    act_e.wait_ge(s_ss, k - 1)
                act_e.activation(sq[:, k % 2, :], x[:, k, :], ACT.Square).then_inc(s_sq, 1)
            for n in range(2):
                hi(n, n, NK)
            act_e.wait_ge(s_eps, 1)
            for L in range(DEPTH):
                act_e.wait_ge(s_mod, L * N_MOD + 2)
                norm(2 * L, L, 0)
                def q_std(e):
                    E = L * NE + e
                    act_e.wait_ge(s_qst, E + 1)
                    if e >= 2:
                        act_e.wait_ge(s_qn, E - 1)
                    act_e.activation(qk_rstd[:, e % 2, :], lin[3], ACT.Sqrt, bias=eps[:, :],
                                     scale=1.0 / HD).then_inc(s_qsd, 1)

                def q_hi(e):
                    act_e.wait_ge(s_qk, L * NE + e + 1)
                    for i in range(2):
                        a = i * HALF
                        act_e.activation(q_st[a:a + HALF, 2 * (e - 1) + i, :], qk[a:a + HALF, e % 3, :],
                                         ACT.Copy).then_inc(s_qs_hi, 1)

                for n in range(N_IN):
                    N = tile_in(L) + n
                    act_e.wait_ge(s_lin, N + 1)
                    e = e_of(n)
                    if e is not None:
                        E = L * NE + e
                        if e >= 2:
                            act_e.wait_ge(s_qst, E - 1)
                        else:
                            act_e.wait_ge(s_ss, (2 * L + 1) * NK)
                        act_e.activation(sq[:, E % 2, :], lin[n % 2], ACT.Square).then_inc(s_qsq, 1)
                        if e == 3:
                            act_e.wait_ge(s_qn, E - 2)
                        elif e > 3:
                            act_e.wait_ge(s_qs, 2 * (L * NQ + e - 3))
                        act_e.activation(qk[:, e % 3, :], lin[n % 2], ACT.Copy).then_inc(s_free, 1)
                    elif n == IN_V:
                        act_e.activation(v_feat[:, :], lin[n % 2], ACT.Copy).then_inc(s_free, 1)
                    hi(N + 2, n % 2, NK)
                    if n > 0 and e_of(n - 1) is not None:
                        q_std(e_of(n - 1))
                    if n == IN_Q + 1:
                        act_e.wait_ge(s_vt, L + 1)
                        if L > 0:
                            act_e.wait_ge(s_out, 16 * 2 * L)
                            act_e.wait_ge(s_o, L * NU)
                        act_e.activation(val[:, :, :], pair[2][:, 0:T].rearrange("p (t c) -> p t c", t=NT),
                                         ACT.Copy).then_inc(s_val, 1)
                        act_e.activation(keys[:, TP:TP + PAST], pair[2][:, T:T + P], ACT.Copy).then_inc(s_pk, 1)
                        act_e.wait_ge(s_val, L + 1)
                        act_e.dma_start(new_v[0, L].rearrange("t h d -> t (h d)"), val[:, 0, :]).then_inc(s_out, 16)
                        act_e.wait_ge(s_qk, L * NE + 1)
                        act_e.wait_ge(s_pk, L + 1)
                        for g in range(KV // HD):
                            for a in (g * HALF, (1 - g) * HALF):
                                act_e.activation(k_hi[a:a + HALF, g, :], keys[g * HALF:(g + 1) * HALF, :],
                                                 ACT.Copy).then_inc(s_ks_hi, 1)
                    if n == IN_Q + 2:
                        act_e.wait_ge(s_kt, L + 1)
                        act_e.activation(k_out[:, :], pair[2][:, T:T + P], ACT.Copy).then_inc(s_kout, 1)
                        act_e.wait_ge(s_kout, L + 1)
                        act_e.dma_start(new_k[0, L].rearrange("t h d -> t (h d)"), k_out[:, :]).then_inc(s_out, 16)
                        q_hi(1)
                    if n == IN_Q + 3:
                        q_hi(2)
                for g in range(NPOOL):
                    act_e.wait_ge(s_pm, L * NPOOL + g + 1)
                    act_e.activation(in_hi[:, NQ + g, :], lin[g % 2], ACT.Copy,
                                     scale=v(L, V_PS, g)).then_inc(s_phi, 1)
                    if g == 1:
                        q_std(NQ)
                q_hi(3)
                for i in range(NU + 2):
                    if i < NU:
                        un = L * NU + i
                        b, h = UNITS[i]
                        nkeys = P if b == 0 else T
                        if i == 2:
                            q_hi(NQ)
                        act_e.wait_ge(s_neg, un + 1)
                        if i >= 2:
                            act_e.wait_ge(s_pt, un - 1)
                        act_e.activation(prob[:, i % 2, 0:nkeys], lin[i % 2][:, 0:nkeys], ACT.Exp,
                                         bias=small[:, i % 2, 0:1], scale=SCALE,
                                         accum_out=small[:, i % 2, 1:2]).then_inc(s_exp, 1)
                    if 1 <= i <= NU:
                        un = L * NU + i - 1
                        nkeys = P if UNITS[i - 1][0] == 0 else T
                        act_e.wait_ge(s_pt, un + 1)
                        if i - 1 >= 2:
                            act_e.wait_ge(s_o, un - 1)
                        act_e.activation(prob_t[:, (i - 1) % 2, 0:nkeys], pair[2][:, 0:nkeys],
                                         ACT.Copy).then_inc(s_pte, 1)
                    if i >= 2 and (i - 1) % NH == 0:
                        pos = (i - 1) // NH - 1
                        b = BLOCKS[pos]
                        act_e.wait_ge(s_o, L * NU + (pos + 1) * NH)
                        act_e.activation(in_hi[:, 0:NQ, b * P:(b + 1) * P], o_bank(pos), ACT.Copy).then_inc(s_ohi, 1)
                up = tile_up(L, 0)
                out = tile_out(L)
                for m in range(N_OUT):
                    N = out + m
                    act_e.wait_ge(s_lin, N + 1)
                    hi(N + 2, m % 2, NK)
                    squares((2 * L + 1) * NK + m, upd_out(L) + m + 1, m)
                norm(2 * L + 1, L, 1)
                act_e.preload_act_table(ACT.Silu)
                for g in range(NG):
                    def up_iter(j, nxt, nk, L=L, g=g):
                        n = (L * NG + g) * FG + j
                        base = tile_up(L, g)
                        for s in range(2):
                            act_e.wait_ge(s_lin, 2 * j + (base + s + 1))
                            if L + g > 0 or not isinstance(j, int) or j > 0:
                                if s == 0:
                                    act_e.wait_ge(s_silu, n)
                                else:
                                    act_e.wait_ge(s_act, n)
                            act_e.activation(conv[:, s, :], lin[s], ACT.Identity, bias=v(L, V_CONVB, s * NF + g * FG + j),
                                             scale=v(L, V_TAP[1], s * NF + g * FG + j)).then_inc(s_ctr, 1)
                            if isinstance(nxt, int):
                                hi(nxt + s, s, nk)
                            else:
                                hi_at(base + 2, j, s, nk)
                        act_e.wait_ge(s_tap, 8 * n + 4)
                        if L + g > 0 or not isinstance(j, int) or j > 0:
                            act_e.wait_ge(s_alo, n)
                        act_e.activation(silu_a[:, :], conv[:, 0, :], ACT.Silu).then_inc(s_silu, 1)
                    up_iter(0, tile_up(L, g) + 2, NK)
                    with act_e.Fori(1, FG - 1) as j:
                        up_iter(j, None, NK)
                    up_iter(FG - 1, tile_down(L, g), FG)

                    last = g == NG - 1 and L == DEPTH - 1
                    down = tile_down(L, g)
                    for m in range(NK):
                        N = down + m
                        act_e.wait_ge(s_lin, N + 1)
                        if N + 2 < DEPTH * PER_LAYER:
                            hi(N + 2, m % 2, FG if m + 2 < NK else NK)
                        if g == NG - 1:
                            squares((2 * L + 2) * NK + m, upd_down(L, g) + m + 1, m)
                            if L == DEPTH - 1:
                                if m >= 2:
                                    act_e.wait_ge(s_yt, m - 1)
                                act_e.activation(yf[:, m % 2, :], x[:, m, :], ACT.Copy,
                                                 scale=v(0, V_FIN, m)).then_inc(s_y, 1)
            act_e.wait_ge(s_stat, 2 * DEPTH + 1)
            act_e.activation(rtok[:, :], pair[0][:, 0:NT], ACT.Sqrt, bias=eps[:, :], scale=1.0 / D).then_inc(s_sd, 1)

        @block.vector
        def _(dve):
            def y_copy(m):
                dve.wait_ge(s_yt, m + 1)
                dve.tensor_copy(yout[:, :, m * P:(m + 1) * P],
                                pair[2 + m % 2][:, 0:T].rearrange("p (t c) -> p t c", t=NT)).then_inc(s_ye, 1)

            def o_low(L, pos):
                b = BLOCKS[pos]
                dve.wait_ge(s_ohi, L * NT + pos + 1)
                dve.tensor_tensor(in_lo[:, 0:NQ, b * P:(b + 1) * P], o_bank(pos),
                                  in_hi[:, 0:NQ, b * P:(b + 1) * P].bitcast(F32), ALU.subtract).then_inc(s_olo, 1)

            def lo(n, s, nk):
                dve.wait_ge(s_whi, n + 1)
                dve.tensor_tensor(w_lo[:, s, 0:nk, :], w_raw[:, s, 0:nk, :], w_hi[:, s, 0:nk, :].bitcast(F32),
                                  ALU.subtract).then_inc(s_wlo, 1)

            def mod_unit(C, k, s):
                if C is None:
                    return
                half = k // 2 if isinstance(k, int) else (k - s) // 2
                mod_unit_at(C, k, s, half, isinstance(k, int) and k == 0)

            def mod_unit_at(C, k, s, half, first):
                if C is None:
                    return
                dve.wait_ge(s_mraw[s], 16 * half + 16 * (unit(C, 0) // 2 + 1))
                if first and C > 2:
                    dve.wait_ge(s_mred, C - 2)
                for ci in range(2):
                    if first:
                        dve.tensor_scalar(mod_acc[:, ci, :], mod_raw[:, s, :], cond[:, ci, 0:1], None,
                                          ALU.mult).then_inc(s_macc, 1)
                    else:
                        dve.wait_ge(s_macc, 2 * k + (2 * unit(C, 0) + ci - 1))
                        dve.scalar_tensor_tensor(out=mod_acc[:, ci, :], in0=mod_raw[:, s, :],
                                                 scalar=cond[:, ci, ds(k, 1)], in1=mod_acc[:, ci, :],
                                                 op0=ALU.mult, op1=ALU.add).then_inc(s_macc, 1)

            def mod_finish(C):
                if C is None:
                    return
                L, ch = C // N_MOD, C % N_MOD
                if C < 2:
                    dve.wait_ge(s_mfirst, NK)
                else:
                    dve.wait_ge(s_mred, C - 1)
                for ci in range(2):
                    if C < 2:
                        sums = pair[C][:, :].rearrange("p (j i r) -> p i j r", j=NK, i=2)[:, ci, :, 0]
                    else:
                        sums = pair[2][:, MODP + ci * NK:MODP + (ci + 1) * NK]
                    ins = dve.tensor_tensor(mod[:, L, ch, ci, :], sums, v(L, V_BMOD, ch * NK, NK), ALU.add)
                ins.then_inc(s_mod, 1)
                if ch % 3 == 1:
                    dve.wait_ge(s_mod, C + 1)
                    for ci in range(2):
                        ins = dve.scalar_tensor_tensor(out=gain[:, L, ch // 3, ci, :], in0=mod[:, L, ch, ci, :],
                                                       scalar=1.0, in1=v(L, (V_N1, V_N2)[ch // 3], 0, NK),
                                                       op0=ALU.add, op1=ALU.mult)
                    ins.then_inc(s_gain, 1)

            def norm(i, L, which):
                dve.wait_ge(s_sd, i + 1)
                dve.reciprocal(rstd[:, :], rstd[:, :]).then_inc(s_rstd, 1)
                dve.wait_ge(s_rstd, i + 1)
                dve.wait_ge(s_gain, 2 * L + which + 1)
                for k in range(NK + 1):
                    if k < NK:
                        for ci, a, b in SEG:
                            if k >= 2:
                                dve.wait_ge(s_h, 2 * (i * NK + k - 2) + 1 + ci)
                            dve.scalar_tensor_tensor(out=norm_t[:, k % 2, a:b], in0=x[:, k, a:b],
                                                     scalar=gain[:, L, which, ci, k:k + 1], in1=rstd[:, a:b],
                                                     op0=ALU.mult, op1=ALU.mult).then_inc(s_nt, 1)
                    if k > 0:
                        for ci, a, b in SEG:
                            dve.wait_ge(s_hhi, 2 * (i * NK + k - 1) + 1 + ci)
                            dve.scalar_tensor_tensor(out=in_lo[:, k - 1, a:b], in0=norm_t[:, (k - 1) % 2, a:b],
                                                     scalar=mod[:, L, 3 * which, ci, k - 1:k],
                                                     in1=in_hi[:, k - 1, a:b].bitcast(F32),
                                                     op0=ALU.add, op1=ALU.subtract).then_inc(s_h, 1)

            def residual(N, s, L, ch, m):
                dve.wait_ge(s_lin, N + 1)
                for ci, a, b in SEG:
                    ins = dve.scalar_tensor_tensor(out=x[:, m, a:b], in0=lin[s][:, a:b],
                                                   scalar=mod[:, L, ch, ci, m:m + 1], in1=x[:, m, a:b],
                                                   op0=ALU.mult, op1=ALU.add)
                ins.then_inc(s_xupd, 1)

            for n in range(2):
                lo(n, n, NK)
            dve.wait_ge(s_vec, 1)
            for C in range(2):
                mod_finish(C)
            for L in range(DEPTH):
                norm(2 * L, L, 0)

                def q_norm(e):
                    E = L * NE + e
                    dve.wait_ge(s_qsd, E + 1)
                    dve.reciprocal(qk_rstd[:, e % 2, :], qk_rstd[:, e % 2, :]).then_inc(s_qrs, 1)
                    dve.wait_ge(s_qrs, E + 1)
                    dve.wait_ge(s_free, L * (N_IN - NPOOL) + E_TILE[e] - IN_K + 1)
                    parts = ((keys[:, 0:TP], 0, TP), (keys[:, TP + PAST:], TP, T)) if e == 0 else ((qk[:, e % 3, :], 0, T),)
                    for d, a, b in parts:
                        ins = dve.scalar_tensor_tensor(out=d, in0=qk[:, e % 3, a:b], scalar=v(L, V_KG if e == 0 else V_QG, 0),
                                                       in1=qk_rstd[:, e % 2, a:b], op0=ALU.mult, op1=ALU.mult)
                    ins.then_inc(s_qn, 1)
                    dve.wait_ge(s_qn, E + 1)
                    if E > 0:
                        dve.wait_ge(s_rp, 2 * E)
                    latent = keys[:, TP + PAST:] if e == 0 else qk[:, e % 3, TP:T]
                    dve.stream_shuffle(rope[:, 0, :], latent, [(i + 16) % 32 for i in range(32)]).then_inc(s_shuf, 1)

                def q_low(e):
                    for i in range(2):
                        a, o = i * HALF, (1 - i) * HALF
                        dve.wait_ge(s_qs_hi, 2 * (L * NQ + e - 1) + i + 1)
                        dve.tensor_tensor(q_st[o:o + HALF, 2 * (e - 1) + i, :], qk[a:a + HALF, e % 3, :],
                                          q_st[a:a + HALF, 2 * (e - 1) + i, :].bitcast(F32),
                                          ALU.subtract).then_inc(s_qs, 1)

                def window_end(g):
                    dve.wait_ge(s_tree, 4 * (L * NPOOL + g + 1))
                    for at, n in ((U_P, TP), (U_S, TS)):
                        ins = dve.scalar_tensor_tensor(out=u[:, g, at:at + n], in0=tree[:, g % 2, at:at + n],
                                                       scalar=1.0 / WINDOWS[g], in1=u[:, g, at:at + n],
                                                       op0=ALU.mult, op1=ALU.subtract)
                    ins.then_inc(s_pooled, 1)

                def pool_low(g):
                    dve.wait_ge(s_phi, L * NPOOL + g + 1)
                    dve.scalar_tensor_tensor(out=in_lo[:, NQ + g, :], in0=lin[g % 2], scalar=v(L, V_PS, g),
                                             in1=in_hi[:, NQ + g, :].bitcast(F32), op0=ALU.mult,
                                             op1=ALU.subtract).then_inc(s_plo, 1)

                units_at = {0: (0, 1), 1: (2, 3), 2: (4,), 3: (5,), 4: (6,), 5: (7,)} if L == 0 else {}
                for n in range(N_IN):
                    N = tile_in(L) + n
                    dve.wait_ge(s_lin, N + 1)
                    if n < NPOOL:
                        if n == 0:
                            dve.wait_ge(s_upad, 3 * (L + 1))
                        dve.tensor_copy(u[:, n, U_P:U_P + TP], lin[n % 2][:, 0:TP]).then_inc(s_u, 1)
                        dve.tensor_copy(u[:, n, U_S:U_S + TS], lin[n % 2][:, TP:T]).then_inc(s_u, 1)
                    lo(N + 2, n % 2, NK)
                    if e_of(n - 1) is not None:
                        q_norm(e_of(n - 1))
                    if 2 <= n < 2 + NPOOL:
                        window_end(n - 2)
                    if n == IN_Q + 1:
                        for g in range(KV // HD):
                            for i, a in enumerate((g * HALF, (1 - g) * HALF)):
                                dve.wait_ge(s_ks_hi, (L * 2 + g) * 2 + 1)
                                own = slice(g * HALF, (g + 1) * HALF)
                                dve.tensor_tensor(k_lo[a:a + HALF, g, :], keys[own, :], k_hi[own, g, :].bitcast(F32),
                                                  ALU.subtract).then_inc(s_ks, 1)
                    if n in (IN_Q + 2, IN_Q + 3):
                        q_low(n - IN_Q - 1)
                    for k in units_at.get(n, ()):
                        mod_unit(2, k, k % 2)
                for g in range(NPOOL):
                    pool_low(g)
                    if g == 1:
                        q_norm(NQ)
                q_low(3)
                if L == 0:
                    mod_finish(2)
                for i in range(NU + 1):
                    if i < NU:
                        un = L * NU + i
                        nkeys = P if UNITS[i][0] == 0 else T
                        dve.wait_ge(s_s, un + 1)
                        dve.tensor_reduce(small[:, i % 2, 3:4], lin[i % 2][:, 0:nkeys], AX_X, ALU.max).then_inc(s_max, 1)
                        dve.wait_ge(s_max, un + 1)
                        if i >= 2:
                            dve.wait_ge(s_exp, un - 1)
                        dve.tensor_scalar(small[:, i % 2, 0:1], small[:, i % 2, 3:4], -SCALE, None,
                                          ALU.mult).then_inc(s_neg, 1)
                    if i > 0:
                        un = L * NU + i - 1
                        nkeys = P if UNITS[i - 1][0] == 0 else T
                        dve.wait_ge(s_exp, un + 1)
                        dve.reciprocal(small[:, (i - 1) % 2, 2:3], small[:, (i - 1) % 2, 1:2]).then_inc(s_rec, 1)
                        dve.wait_ge(s_rec, un + 1)
                        dve.tensor_scalar(prob[:, (i - 1) % 2, 0:nkeys], prob[:, (i - 1) % 2, 0:nkeys],
                                          small[:, (i - 1) % 2, 2:3], None, ALU.mult).then_inc(s_prob, 1)
                    if i == 2:
                        q_low(NQ)
                    if i >= 3 and (i - 2) % NH == 0:
                        o_low(L, (i - 2) // NH - 1)
                    if L == 0 and i >= 4 and i % 4 == 0 and i < 4 + 4 * NK:
                        mod_unit(3, i // 4 - 1, (i // 4 - 1) % 2)
                o_low(L, NT - 1)
                for m in range(N_OUT):
                    N = tile_out(L) + m
                    if m == 0:
                        dve.wait_ge(s_mod, L * N_MOD + 3)
                    residual(N, m % 2, L, 2, m)
                    lo(N + 2, m % 2, NK)
                    if L == 0 and m == 1:
                        mod_finish(3)
                    if L == 0 and 1 <= m <= 4:
                        for s in range(2):
                            mod_unit(4, 2 * (m - 1) + s, s)
                    if L == 0 and m == 6:
                        mod_finish(4)
                norm(2 * L + 1, L, 1)
                for g in range(NG):
                    base = tile_up(L, g)

                    A, B, C = mlp_chunks(L, g)

                    def up_iter(j, nxt, nk, chunk=None, j0=0, L=L, g=g, base=base):
                        n = (L * NG + g) * FG + j
                        for s in range(2):
                            dve.wait_ge(s_ctr, 2 * n + s + 1)
                            tap = 4 * (2 * n + s)
                            for r, (t, sh) in enumerate(((0, -1), (2, 1))):
                                for ci, a, b in SEG:
                                    d0, d1 = (a + 1, b) if sh < 0 else (a, b - 1)
                                    if r == 1:
                                        dve.wait_ge(s_tap, tap + ci + 1)
                                    ins = dve.scalar_tensor_tensor(
                                        out=conv[:, s, d0:d1], in0=lin[s][:, d0 + sh:d1 + sh],
                                        scalar=v(L, V_TAP[t], s * NF + g * FG + j), in1=conv[:, s, d0:d1],
                                        op0=ALU.mult, op1=ALU.add).then_inc(s_tap, 1)
                            if isinstance(nxt, int):
                                lo(nxt + s, s, nk)
                            else:
                                lo(2 * j + (base + 2 + s), s, nk)
                            mod_unit_at(chunk, 2 * j + (s - 2 * j0), s, j - j0, isinstance(j, int) and j == j0 and s == 0)
                    up_iter(0, base + 2, NK, A)
                    with dve.Fori(1, 4) as j:
                        up_iter(j, None, NK, A)
                    with dve.Fori(4, 6) as j:
                        up_iter(j, None, NK)
                    mod_finish(A)
                    up_iter(6, base + 14, NK, B, 6)
                    with dve.Fori(7, FG - 1) as j:
                        up_iter(j, None, NK, B, 6)
                    up_iter(FG - 1, base + 2 * FG, FG)
                    down = tile_down(L, g)
                    mod_finish(B)
                    dve.wait_ge(s_mod, (L + 1) * N_MOD)
                    for m in range(NK):
                        residual(down + m, m % 2, L, 5, m)
                        if down + m + 2 < DEPTH * PER_LAYER:
                            lo(down + m + 2, m % 2, FG if m + 2 < NK else NK)
                        if 1 <= m <= 4:
                            for s in range(2):
                                mod_unit(C, 2 * (m - 1) + s, s)
                        if m == 6:
                            mod_finish(C)
                        if L == DEPTH - 1 and g == NG - 1 and m > 0:
                            y_copy(m - 1)
            y_copy(NK - 1)
            dve.wait_ge(s_sd, 2 * DEPTH + 1)
            dve.reciprocal(rtok[:, :], rtok[:, :]).then_inc(s_rstd, 1)
            dve.wait_ge(s_rstd, 2 * DEPTH + 1)
            dve.wait_ge(s_ye, NK)
            for b in range(NT):
                dve.tensor_scalar(yout[:, b, :], yout[:, b, :], rtok[:, b:b + 1], None, ALU.mult).then_inc(s_yn, 1)

        @block.tensor
        def _(pe):
            def split_matmul(dst, s, k, rhs_hi, rhs_lo, kk, first, last):
                passes = ((w_hi, rhs_hi), (w_hi, rhs_lo), (w_lo, rhs_hi))
                for r, (w, rhs) in enumerate(passes):
                    for hf in range(2):
                        a = hf * HALF_T
                        ins = pe.matmul(dst[:, a:a + HALF_T], w[:, s, k, :], rhs[:, kk, a:a + HALF_T],
                                        start=first and r == 0, stop=last and r == 2)
                return ins

            def linear(n, s, nk, rhs_hi, rhs_lo, wait_k=None):
                pe.wait_ge(s_wlo, n + 1)
                for k in range(nk):
                    if wait_k is not None:
                        wait_k(k)
                    ins = split_matmul(lin[s], s, k, rhs_hi, rhs_lo, k, k == 0, k == nk - 1)
                ins.then_inc(s_lin, 1)

            def linear_pair(n, nk, rhs_hi, rhs_lo, wait_k=None, order=None):
                pe.wait_ge(s_wlo, n + 2)
                order = list(order or range(nk))
                for r, k in enumerate(order):
                    if wait_k is not None:
                        wait_k(k)
                    for s in range(2):
                        ins = split_matmul(lin[s], s, k, rhs_hi, rhs_lo, k, r == 0, r == nk - 1)
                        if r == nk - 1:
                            ins.then_inc(s_lin, 1)

            def stat(i):
                pe.wait_ge(s_ss, (i + 1) * NK)
                if i % 2 == 1:
                    pe.wait_ge(s_olo, (i // 2 + 1) * NT)
                for hf in range(2):
                    a = hf * HALF_T
                    ins = pe.matmul(lin[3][:, a:a + HALF_T], ones, ssum[:, a:a + HALF_T], start=True, stop=True)
                ins.then_inc(s_stat, 1)

            def mod_reduce(C):
                if C is None:
                    return
                pe.wait_ge(s_macc, 2 * unit(C, NK))
                pe.wait_ge(s_mod, C)
                for r in range(2 * NK):
                    ins = pe.matmul(pair[2][:, MODP + r:MODP + r + P], mod_acc[:, r // NK, (r % NK) * P:(r % NK + 1) * P],
                                    ones, start=True, stop=True)
                ins.then_inc(s_mred, 1)

            def y_transpose(m):
                pe.wait_ge(s_y, m + 1)
                if m >= 2:
                    pe.wait_ge(s_ye, m - 1)
                for b in range(NT):
                    ins = pe.transpose(pair[2 + m % 2][:, b * P:(b + 1) * P], yf[:, m % 2, b * P:(b + 1) * P], ident)
                ins.then_inc(s_yt, 1)

            def h_wait(i):
                return lambda k: pe.wait_ge(s_h, 2 * (i * NK + k + 1))

            def mod_first(k):
                pe.wait_ge(s_first[k], 16)
                rhs = cond[:, :, k:k + 1].to_broadcast([P, 2, HALF])
                for j in range(2 * NK):
                    a = j % NK * P
                    ins = pe.matmul(pair[j // NK][:, a:a + P].rearrange("p (i r) -> p i r", i=2),
                                    w_first[:, k % N_FIRST, j * P:(j + 1) * P], rhs,
                                    start=k == 0 and j % 4 == 0, stop=k == NK - 1, skip_group_check=True)
                ins.then_inc(s_mfirst, 1)

            pe.wait_ge(s_const0, 16)
            pe.wait_ge(s_crow, 16 * 2)
            pe.transpose(pair[2][:, 0:2 * NK], cond_rows[:, :], ident[0:2 * NK, 0:2 * NK]).then_inc(s_vec_t, 1)
            pe.wait_ge(s_cond, 1)
            N_ROW_DMAS = 5 + 4 + 3 + DEPTH
            pe.wait_ge(s_rows, 16 * N_ROW_DMAS)
            for L in range(DEPTH):
                if L > 0:
                    pe.wait_ge(s_vec, L)
                for t in range(3):
                    ins = pe.transpose(pair[2][:, t * P:t * P + N_ROWS[t]], rows[0:N_ROWS[t], L, t, :],
                                       ident[0:N_ROWS[t], 0:N_ROWS[t]])
                ins.then_inc(s_vec_t, 1)
            for k in range(4):
                mod_first(k)
            pe.wait_ge(s_x, 32)
            pe.wait_ge(s_vec, DEPTH)
            for k in range(NK):
                if k >= 2:
                    pe.wait_ge(s_xe, k - 1)
                for b in range(NT):
                    ins = pe.transpose(pair[2 + k % 2][:, b * P:(b + 1) * P], xin[:, b, k * P:(k + 1) * P], ident)
                ins.then_inc(s_xt, 1)
            for k in range(4, NK):
                mod_first(k)
            pe.wait_ge(s_const, 16)
            pe.wait_ge(s_xe, NK)
            stat(0)

            def q_stat(E):
                pe.wait_ge(s_qsq, E + 1)
                if E % NE > 0:
                    pe.wait_ge(s_qsd, E)
                for hf in range(2):
                    a = hf * HALF_T
                    ins = pe.matmul(lin[3][:, a:a + HALF_T], head_ones, sq[:, E % 2, a:a + HALF_T], start=True, stop=True)
                ins.then_inc(s_qst, 1)

            for L in range(DEPTH):
                if L == 0:
                    pe.wait_ge(s_mod, 2)
                else:
                    pe.wait_ge(s_xupd, upd_down(L - 1, NG - 1) + NK)
                linear_pair(tile_in(L), NK, in_hi, in_lo, h_wait(2 * L))
                for n in range(2, N_IN):
                    if n - 2 < IN_K:
                        pe.wait_ge(s_u, 2 * (L * NPOOL + n - 1))
                    else:
                        pe.wait_ge(s_free, L * (N_IN - NPOOL) + n - 1 - IN_K)
                    linear(tile_in(L) + n, n % 2, NK, in_hi, in_lo)
                    if n > 0 and e_of(n - 1) is not None:
                        if n == IN_V:
                            pe.wait_ge(s_sd, 2 * L + 1)
                        q_stat(L * NE + e_of(n - 1))
                    if n == IN_Q:
                        pe.wait_ge(s_free, L * (N_IN - NPOOL) + IN_V - IN_K + 1)
                        pe.wait_ge(s_past, 32 * (L + 1))
                        for b in range(NT):
                            pe.transpose(pair[2][:, b * P:(b + 1) * P], v_feat[:, b * P:(b + 1) * P], ident)
                        pe.transpose(pair[2][:, T:T + P], past[:, 0, :], ident).then_inc(s_vt, 1)
                    if n == IN_Q + 2:
                        pe.wait_ge(s_pk, L + 1)
                        pe.wait_ge(s_qn, L * NE + 1)
                        pe.transpose(pair[2][:, T:T + P], keys[:, 0:P], ident).then_inc(s_kt, 1)
                pe.wait_ge(s_wp, 16 * (L + 1))
                for g in range(NPOOL):
                    pe.wait_ge(s_pooled, L * NPOOL + g + 1)
                    if g < 2:
                        pe.wait_ge(s_free, L * (N_IN - NPOOL) + N_IN - 1 + g - IN_K)
                    else:
                        pe.wait_ge(s_plo, L * NPOOL + g - 1)
                    d = lin[g % 2]
                    pe.matmul(d[:, 0:TP], wp[:, g, :], u[:, g, U_P:U_P + TP], start=True, stop=True)
                    cut = HALF_T - TP
                    pe.matmul(d[:, TP:HALF_T], wp[:, g, :], u[:, g, U_S:U_S + cut], start=True, stop=True)
                    pe.matmul(d[:, HALF_T:T], wp[:, g, :], u[:, g, U_S + cut:U_S + TS], start=True,
                              stop=True).then_inc(s_pm, 1)
                    if g == 1:
                        q_stat(L * NE + NQ)
                if L == 0:
                    mod_reduce(2)

                def scores(i):
                    b, h = UNITS[i]
                    un = L * NU + i
                    if i < 2:
                        pe.wait_ge(s_plo, L * NPOOL + NPOOL - 1 + i)
                        pe.wait_ge(s_ks, 4 * (L + 1))
                    else:
                        pe.wait_ge(s_exp, un - 1)
                    pe.wait_ge(s_qs, 2 * L * NQ + h + 1)
                    runs = ((0, 0, 2 * P),) if b == 0 else tuple((TP + hf * HALF_T, hf * HALF_T, HALF_T) for hf in range(2))
                    for kc, oc, n in runs:
                        for r, kk in enumerate((k_hi, k_lo)):
                            ins = pe.matmul(lin[i % 2][:, oc:oc + n], q_st[:, h, b * P:(b + 1) * P],
                                            kk[:, h // GRP, kc:kc + n], start=r == 0, stop=r == 1)
                    ins.then_inc(s_s, 1)

                def transpose_prob(i):
                    un = L * NU + i
                    pe.wait_ge(s_prob, un + 1)
                    if i > 0:
                        pe.wait_ge(s_pte, un)
                    else:
                        pe.wait_ge(s_val, L + 1)
                        pe.wait_ge(s_kout, L + 1)
                    for kt in range(1 if UNITS[i][0] == 0 else NT):
                        ins = pe.transpose(pair[2][:, kt * P:(kt + 1) * P], prob[:, i % 2, kt * P:(kt + 1) * P], ident)
                    ins.then_inc(s_pt, 1)

                def weigh(i):
                    b, h = UNITS[i]
                    pos = i // NH
                    un = L * NU + i
                    a = (h % 2) * HALF
                    g = h // GRP
                    pe.wait_ge(s_pte, un + 1)
                    if h == 0:
                        if pos >= 2:
                            pe.wait_ge(s_olo, L * NT + pos - 1)
                        if pos == 0:
                            pe.wait_ge(s_qsd, (L + 1) * NE)
                    dst = pair[3][a:a + HALF, (pos % 2) * 512 + h // 2 * P:(pos % 2) * 512 + (h // 2 + 1) * P]
                    nkt = 1 if b == 0 else NT
                    for kt in range(nkt):
                        vv = val[:, 0, g * HD:(g + 1) * HD] if b == 0 else \
                            past[:, 1, g * HD:(g + 1) * HD] if kt == 0 else val[:, kt, g * HD:(g + 1) * HD]
                        ins = pe.matmul(dst, vv, prob_t[:, i % 2, kt * P:(kt + 1) * P], start=kt == 0, stop=kt == nkt - 1)
                    ins.then_inc(s_o, 1)

                scores(0)
                scores(1)
                for i in range(NU):
                    if i + 2 < NU:
                        scores(i + 2)
                    if i > 0:
                        weigh(i - 1)
                    transpose_prob(i)
                weigh(NU - 1)
                for i in range(2):
                    pe.wait_ge(s_exp, (L + 1) * NU - 1 + i)

                def out_wait(k):
                    if k == 0:
                        pe.wait_ge(s_olo, (L + 1) * NT)
                linear_pair(tile_out(L), NK, in_hi, in_lo, out_wait, list(range(NQ, NK)) + list(range(NQ)))
                for m in range(2, N_OUT):
                    if m == 2 and L == 0:
                        mod_reduce(3)
                    pe.wait_ge(s_xupd, upd_out(L) + m - 1)
                    linear(tile_out(L) + m, m % 2, NK, in_hi, in_lo)
                    if m == 5 and L == 0:
                        mod_reduce(4)
                stat(2 * L + 1)
                for g in range(NG):
                    base = tile_up(L, g)
                    A, B, C = mlp_chunks(L, g)

                    def up_iter(j, L=L, g=g, base=base):
                        for s in range(2):
                            pe.wait_ge(s_tap, 8 * j + (8 * (L * NG + g) * FG - 4 + 4 * s))
                            linear(2 * j + (base + s), s, NK, in_hi, in_lo)
                    pe.wait_ge(s_xupd, (upd_out(L) if g == 0 else upd_down(L, g - 1)) + NK)
                    linear_pair(base, NK, in_hi, in_lo, h_wait(2 * L + 1) if g == 0 else None)
                    with pe.Fori(1, 5) as j:
                        up_iter(j)
                    mod_reduce(A)
                    with pe.Fori(5, FG) as j:
                        up_iter(j)
                    mod_reduce(B)
                    down = tile_down(L, g)
                    done = (L * NG + g) * FG

                    def down_iter(i, L=L, g=g, down=down):
                        for s in range(2):
                            pe.wait_ge(s_xupd, upd_down(L, g) + 2 * i + (s - 1))
                            linear(2 * i + (down + s), s, FG, act_hi, act_lo)
                    pe.wait_ge(s_tap, 8 * (done + FG))
                    linear_pair(down, FG, act_hi, act_lo, lambda k: pe.wait_ge(s_alo, done + k + 1))
                    if L == DEPTH - 1 and g == NG - 1:
                        for m in range(2, NK):
                            pe.wait_ge(s_xupd, upd_down(L, g) + m - 1)
                            linear(down + m, m % 2, FG, act_hi, act_lo)
                            y_transpose(m - 2)
                    else:
                        with pe.Fori(1, NK // 2 - 1) as i:
                            down_iter(i)
                        mod_reduce(C)
                        down_iter(NK // 2 - 1)
                        if g == NG - 1:
                            stat(2 * L + 2)
            y_transpose(NK - 2)
            pe.wait_ge(s_ss, (2 * DEPTH + 1) * NK)
            pe.wait_ge(s_xupd, upd_down(DEPTH - 1, NG - 1) + NK)
            for b in range(NT):
                ins = pe.matmul(pair[0][:, b:b + P], ssum[:, b * P:(b + 1) * P], ones, start=True, stop=True)
            ins.then_inc(s_stat, 1)
            y_transpose(NK - 1)


_INS = ['x_prompt', 'x_sample', 'cache_k', 'cache_v', 'c', 'c_ctx', 'w_mod', 'b_mod', 'norm1_g', 'w_in', 'q_norm_g',
        'k_norm_g', 'w_pool', 'pool_scale', 'w_out', 'norm2_g', 'w_up', 'conv_w', 'conv_b', 'w_down', 'final_norm_g']


def kernel(**inputs):
    import numpy as _np
    import concourse.bacc as _bacc
    from concourse import mybir as _mybir
    from concourse.bass_utils import run_bass_kernel_spmd as _run

    nc = _bacc.Bacc("TRN2", target_bir_lowering=False, num_devices=1)
    arrays, args = {}, []
    for name in _INS:
        arrays[f"in_{name}_dram"] = _np.ascontiguousarray(inputs[name])
    b, s, d = inputs['x_prompt'].shape
    db, ds_, _ = inputs['x_sample'].shape
    depth = inputs['w_in'].shape[0]
    kvh, hd = inputs['cache_k'].shape[3:]
    arrays["in_consts_dram"] = shape_constants(s, ds_, hd)
    for name, a in arrays.items():
        args.append(nc.dram_tensor(name, a.shape, _mybir.dt.from_np(a.dtype), kind="ExternalInput").ap())
    outs = [(b, s, d), (db, ds_, d), (b, depth, s, kvh, hd), (b, depth, s, kvh, hd)]
    for i, shape in enumerate(outs):
        args.append(nc.dram_tensor(f"out_{i}_dram", shape, _mybir.dt.float32, kind="ExternalOutput").ap())
    build(nc, *args)
    r = _run(nc, [arrays], core_ids=[0])
    return tuple(r.results[0][f"out_{i}_dram"] for i in range(len(outs)))
```

```python
from contextlib import ExitStack

import numpy as np

import concourse.bass as bass
from concourse import mybir

F32 = mybir.dt.float32
F32R = mybir.dt.float32r
ALU = mybir.AluOpType
ACT = mybir.ActivationFunctionType
AX_X = mybir.AxisListType.X

P = 128
HALF = P // 2
EPS = 1e-6
GRID_W = 64
ROPE_THETA = 10000.0
WINDOWS = (2, 4, 8, 16)
PAD = max(WINDOWS) // 2


def ds(start, size):
    return bass.ds(start, size)


def shape_constants(n_prompt, n_sample, head_dim):
    ident = np.eye(P, dtype=np.float32)
    block = np.kron(np.eye(P // head_dim), np.ones((head_dim, head_dim))).astype(np.float32)
    ones = np.ones((P, P), np.float32)
    quarter = head_dim // 4
    inv = (np.float32(ROPE_THETA) ** (-np.arange(quarter, dtype=np.float32) / np.float32(quarter))).astype(np.float32)
    t = np.arange(n_sample)
    where = np.stack([t // GRID_W, t % GRID_W]).astype(np.float32)
    d = np.arange(P) % head_dim
    axis, second, freq = d // (2 * quarter), (d // quarter) % 2, d % quarter
    angle = (where[axis] * inv[freq][:, None]).astype(np.float32)
    sign = np.where(second == 1, 1.0, -1.0)[:, None]
    edges = np.ones((len(WINDOWS), 2, 2, PAD), np.float32)
    for g, w in enumerate(WINDOWS):
        for s, n in enumerate((n_prompt, n_sample)):
            at = np.concatenate([np.arange(PAD), np.arange(n - PAD, n)])
            count = np.clip(at + w - w // 2, 0, n) - np.clip(at - w // 2, 0, n)
            edges[g, s] = (w / count).reshape(2, PAD)
    return np.concatenate([
        ident, block, ones, np.cos(angle), (np.sin(angle) * sign),
        np.broadcast_to(edges.reshape(1, -1), (P, edges.size))], axis=1).astype(np.float32)


def build(nc, x_prompt, x_sample, cache_k, cache_v, c, c_ctx, w_mod, b_mod, norm1_g, w_in,
          q_norm_g, k_norm_g, w_pool, pool_scale, w_out, norm2_g, w_up, conv_w, conv_b,
          w_down, final_norm_g, consts, y_prompt, y_sample, new_k, new_v):
    DEPTH, D, IN_WIDTH = w_in.shape
    TP, TS = x_prompt.shape[1], x_sample.shape[1]
    T = TP + TS
    HALF_T = T // 2
    PAST = cache_k.shape[2]
    HD = cache_k.shape[4]
    KV = cache_k.shape[3] * HD
    NPOOL = w_pool.shape[1]
    AW = D - NPOOL * P
    NH = AW // HD
    GRP = NH // cache_k.shape[3]
    FF = w_down.shape[1]
    NK = D // P
    NT = T // P
    NQ = AW // P
    NF = FF // P
    NG = 2
    FG = NF // NG
    N_MOD = 6
    SCALE = float(HD) ** -0.5
    assert TP == P and TS % P == 0 and KV == P and PAST == P and NF % NG == 0 and HALF_T % 2 == 0
    SEG = ((0, 0, TP), (1, TP, T))

    N_IN, N_OUT = IN_WIDTH // P, NK
    PER_GROUP = 2 * FG + NK
    PER_LAYER = N_IN + N_OUT + NG * PER_GROUP
    IN_U, IN_K, IN_V, IN_Q = 0, NPOOL, NPOOL + 1, NPOOL + 2
    IN_COLUMN = [AW + 2 * KV + P * g for g in range(NPOOL)] + [AW, AW + KV] + [P * t for t in range(NQ)]
    NE = 1 + NQ
    E_TILE = [IN_K] + [IN_Q + t for t in range(NQ)]

    def tile_in(L):
        return L * PER_LAYER

    def tile_out(L):
        return tile_in(L) + N_IN

    def tile_up(L, g):
        return tile_out(L) + N_OUT + g * PER_GROUP

    def tile_down(L, g):
        return tile_up(L, g) + 2 * FG

    THIRD = [t + 2 for L in range(DEPTH) for t in (tile_in(L), tile_up(L, 0))]

    BLOCKS = [1, 0] + list(range(2, NT))
    UNITS = [(b, h) for b in BLOCKS for h in range(NH)]
    NU = len(UNITS)

    with ExitStack() as ctx:
        def sb(name, shape, dt=F32, at=ctx):
            return at.enter_context(nc.sbuf_tensor(name, shape, dt))

        def sem(name):
            return ctx.enter_context(nc.semaphore(name))

        x = sb("x", [P, NK, T])
        w_raw = sb("w_raw", [P, 2, FG, P])
        w_hi = sb("w_hi", [P, 2, FG, P], F32R)
        w_lo = sb("w_lo", [P, 2, FG, P], F32R)
        mod_raw = sb("mod_raw", [P, 2, D])
        mod_acc = sb("mod_acc", [P, 2, D])
        n_const = consts.shape[1]
        cst = sb("cst", [P, n_const])
        ident, head_ones, ones = (cst[:, i * P:(i + 1) * P] for i in range(3))
        cos, sin = (cst[:, 3 * P + i * TS:3 * P + (i + 1) * TS] for i in range(2))
        edge = cst[:, 3 * P + 2 * TS:n_const].rearrange("p (g s e c) -> p g s e c", g=NPOOL, s=2, e=2)
        vec = sb("vec", [P, DEPTH, 3, P])
        mod = sb("mod", [P, DEPTH, N_MOD, 2, NK])
        gain = sb("gain", [P, DEPTH, 2, 2, NK])
        cond = sb("cond", [P, 2, NK])
        eps = sb("eps", [P, 2])
        wp = sb("wp", [P, NPOOL, P])
        past = sb("past", [P, 2, P])
        val = sb("val", [P, NT, P])
        k_out = sb("k_out", [P, P])
        sq = sb("sq", [P, 2, T])
        ssum = sb("ssum", [P, T])
        v_feat = sb("v_feat", [P, T])
        prob = [sq[:, 0, :], sq[:, 1, :], v_feat[:, :]]
        small = sb("small", [P, 3, 4])
        rtok = sb("rtok", [P, NT])
        rq = sb("rq", [P, 2, NQ * NT * 2])

        with ExitStack() as inputs:
            in_hi = sb("in_hi", [P, NK, T], F32R, at=inputs)
            in_lo = sb("in_lo", [P, NK, T], F32R, at=inputs)
            with ExitStack() as own:
                xin = sb("xin", [P, NT, D], at=own)
                rows = sb("rows", [P, DEPTH, 3, P], at=own)
                cond_rows = sb("cond_rows", [2 * NK, P], at=own)
                N_FIRST = 6
                w_first = sb("w_first", [P, N_FIRST, 2 * D], at=own)
            with ExitStack() as own:
                norm_t = sb("norm_t", [P, 2, T], at=own)
            with ExitStack() as own:
                qk = sb("qk", [P, 3, T], at=own)
                k_rstd = sb("k_rstd", [P, T], at=own)
                keys = sb("keys", [P, T + PAST], at=own)
                q_st = sb("q_st", [P, NH, T], F32R, at=own)
                k_hi = sb("k_hi", [P, KV // HD, T + PAST], F32R, at=own)
                k_lo = sb("k_lo", [P, KV // HD, T + PAST], F32R, at=own)
                rope = sb("rope", [P, 2, TS], at=own)
                prob_t = sb("prob_t", [P, 2, T], at=own)
                w_third_in = k_hi[:, :, :].rearrange("p g t -> p (g t)")[:, 0:NK * P].rearrange("p (k n) -> p k n", k=NK)
                U_P, U_S = PAD, TP + 2 * PAD
                U_W = U_S + TS + PAD
                u = sb("u", [P, NPOOL, U_W], at=own)
                tree = sb("tree", [P, 2, U_W], at=own)
            with ExitStack() as own:
                conv = sb("conv", [P, 2, T], at=own)
                act_hi = sb("act_hi", [P, FG, T], F32R, at=own)
                act_lo = sb("act_lo", [P, FG, T], F32R, at=own)
                silu_a = sb("silu_a", [P, T], at=own)
                w_third = sb("w_third", [P, NK, P], F32R, at=own)
        with ExitStack() as own:
            yout = sb("yout", [P, NT, D], at=own)
            yf = sb("yf", [P, 2, T], at=own)

        pair = [ctx.enter_context(nc.psum_tensor(f"pair{i}", [P, 2 * 512], F32)) for i in range(4)]
        LIN0 = 512 - HALF_T
        lin = [pair[i][:, LIN0:LIN0 + T] for i in range(4)]
        MODP = 832

        V_BMOD, V_CONVB, V_N1, V_N2, V_PS, V_QG, V_KG = (0, 0), (0, 48), (0, 92), (0, 100), (0, 108), (0, 112), (0, 113)
        V_TAP = ((1, 0), (1, NF * 2), (2, 0))
        V_FIN = (2, 44)
        N_ROWS = (114, 88, 52)
        assert 2 * NF == 44 and NK == 8

        def v(L, place, i, n=1):
            return vec[:, L, place[0], ds(place[1] + i, n)]

        s_const, s_rows, s_x = sem("const_loaded"), sem("rows_loaded"), sem("x_loaded")
        s_crow = sem("cond_rows_loaded")
        s_vec_t, s_vec = sem("vec_transposed"), sem("vec_ready")
        s_cond, s_eps = sem("cond_ready"), sem("eps_ready")
        s_xt, s_xe = sem("x_transposed"), sem("x_evacuated")
        s_raw = [sem(f"w_loaded{i}") for i in range(2)]
        s_whi, s_wlo = sem("w_hi_ready"), sem("w_lo_ready")
        s_lin, s_free = sem("lin_done"), sem("lin_free")
        s_gain, s_mfirst = sem("gain_ready"), sem("first_used")
        s_mraw = [sem(f"mod_loaded{i}") for i in range(2)]
        s_macc, s_mred, s_mod = sem("mod_accumulated"), sem("mod_reduced"), sem("mod_ready")
        s_xupd, s_sq, s_ss, s_ss0 = sem("x_updated"), sem("squares_ready"), sem("squares_summed"), sem("sum_cleared")
        s_stat, s_sd, s_rstd, s_bc = sem("stat_done"), sem("std_ready"), sem("rstd_ready"), sem("rstd_spread")
        s_nt, s_hhi, s_h = sem("normed"), sem("h_hi_ready"), sem("h_ready")
        s_qsq, s_qst, s_qsd, s_qrs = sem("qk_squared"), sem("qk_stat"), sem("qk_std"), sem("qk_rstd_ready")
        s_nrq, s_kn, s_shuf = sem("rq_negated"), sem("key_normed"), sem("qk_shuffled")
        s_rp, s_qk = sem("rope_part"), sem("qk_ready")
        s_vf, s_vt, s_val, s_pkt, s_pk = sem("v_copied"), sem("v_transposed"), sem("values_ready"), sem("past_transposed"), sem("past_key_ready")
        s_kt, s_kout = sem("new_key_transposed"), sem("new_key_copied")
        s_past, s_wp = sem("past_loaded"), sem("w_pool_loaded")
        s_out = sem("outputs_written")
        s_upad, s_u, s_tree, s_tstep, s_pooled = sem("pads_cleared"), sem("u_ready"), sem("window_sums"), sem("tree_step"), sem("pooled")
        s_pm, s_phi, s_plo = sem("pool_mixed"), sem("pool_hi"), sem("pool_lo")
        s_qs_hi, s_qs, s_ks_hi, s_ks = sem("query_hi"), sem("query_split"), sem("key_hi"), sem("keys_split")
        s_first, s_const0 = [sem(f"first_loaded{i}") for i in range(8)], sem("ident_loaded")
        s_s, s_max, s_neg, s_exp, s_rec, s_prob = sem("scores_done"), sem("max_ready"), sem("neg_max_ready"), sem("exp_done"), sem("reciprocal_ready"), sem("prob_ready")
        s_pt, s_pte, s_o, s_ohi, s_olo = sem("prob_transposed"), sem("prob_t_ready"), sem("head_done"), sem("o_hi"), sem("o_lo")
        s_ctr, s_tap, s_silu = sem("conv_centre"), sem("conv_tap"), sem("silu_ready")
        s_act, s_ahi, s_alo = sem("act_ready"), sem("act_hi_ready"), sem("act_lo_ready")
        s_y, s_yt, s_ye, s_yn = sem("y_gained"), sem("y_transposed"), sem("y_copied"), sem("y_normed")

        block = ctx.enter_context(nc.Block())

        w_in_v = [w_in[L].rearrange("(k p) n -> p k n", p=P) for L in range(DEPTH)]
        w_out_v = [w_out[L].rearrange("(k p) n -> p k n", p=P) for L in range(DEPTH)]
        w_up_v = [w_up[L].rearrange("(k p) n -> p k n", p=P) for L in range(DEPTH)]
        w_down_v = [w_down[L].rearrange("(k p) n -> p k n", p=P) for L in range(DEPTH)]

        def unit(C, k):
            return (C - 2) * NK + k

        def mlp_chunks(L, g):
            first = L * N_MOD + 5 + 3 * g
            return [C if C < DEPTH * N_MOD else None for C in range(first, first + 3)]

        def o_bank(pos):
            return pair[3][:, (pos % 2) * 512:(pos % 2) * 512 + NQ * P].rearrange("p (t c) -> p t c", t=NQ)

        def rq_of(sign, i):
            b, h = UNITS[i]
            at = (h // 2 * NT + b) * 2 + h % 2
            return rq[:, sign, at:at + 1]

        def up_result(g, j, s):
            return lin[2 + s if g == 0 and isinstance(j, int) and j == 1 else s]

        def e_of(n):
            return E_TILE.index(n) if n in E_TILE else None

        def upd_out(L):
            return L * (1 + NG) * NK

        def upd_down(L, g):
            return upd_out(L) + (1 + g) * NK

        
        @block.sync
        def _(sp):
            def load_w(n, s, src, nk):
                if not isinstance(n, int) or n >= 2:
                    sp.wait_ge(s_wlo, n - 1)
                sp.dma_start(w_raw[:, s, 0:nk, :], src).then_inc(s_raw[s], 16)

            def load_mod(C, k, s):
                if C is None:
                    return
                if not isinstance(k, int) or unit(C, k) >= 2:
                    sp.wait_ge(s_macc, 2 * k + (2 * unit(C, 0) - 2))
                L, ch = C // N_MOD, C % N_MOD
                sp.dma_start(mod_raw[:, s, :], w_mod[L, ds(k * P, P), ch * D:(ch + 1) * D]).then_inc(s_mraw[s], 16)

            def load_first(k):
                if k >= N_FIRST:
                    sp.wait_ge(s_mfirst, k - N_FIRST + 1)
                sp.dma_start(w_first[:, k % N_FIRST, :], w_mod[0, k * P:(k + 1) * P, 0:2 * D]).then_inc(s_first[k], 16)

            def load_in(L, n):
                load_w(tile_in(L) + n, n % 2, w_in_v[L][:, :, IN_COLUMN[n]:IN_COLUMN[n] + P], NK)

            def load_out(L, m):
                load_w(tile_out(L) + m, m % 2, w_out_v[L][:, :, m * P:(m + 1) * P], NK)

            sp.dma_start(ident, consts[:, 0:P]).then_inc(s_const0, 16)
            for i, src in enumerate((c_ctx, c.rearrange("a d -> (a d)"))):
                sp.dma_start(cond_rows[i * NK:(i + 1) * NK, :], src.rearrange("(r c) -> r c", c=P)).then_inc(s_crow, 16)
            for src, at, n, t in ((b_mod, 0, 48, 0), (conv_b, 48, 44, 0), (norm1_g, 92, NK, 0), (norm2_g, 100, NK, 0),
                                  (pool_scale, 108, NPOOL, 0)):
                sp.dma_start(rows[at:at + n, :, t, :], src.rearrange("l (r c) -> r l c", c=P)).then_inc(s_rows, 16)
            for src, at in ((q_norm_g, 112), (k_norm_g, 113)):
                for i in range(2):
                    sp.dma_start(rows[at:at + 1, :, 0, i * HD:(i + 1) * HD],
                                 src.rearrange("l (r c) -> r l c", r=1)).then_inc(s_rows, 16)
            for tap, (t, at) in enumerate(V_TAP):
                sp.dma_start(rows[at:at + 2 * NF, :, t, :],
                             conv_w[:, tap, :].rearrange("l (r c) -> r l c", c=P)).then_inc(s_rows, 16)
            for L in range(DEPTH):
                sp.dma_start(rows[44:44 + NK, L, 2, :], final_norm_g.rearrange("(r c) -> r c", c=P)).then_inc(s_rows, 16)
            for k in range(4):
                load_first(k)
            sp.dma_start(xin[:, 0, :], x_prompt[0]).then_inc(s_x, 16)
            sp.dma_start(xin[:, 1:NT, :], x_sample[0].rearrange("(t p) d -> p t d", p=P)).then_inc(s_x, 16)
            sp.dma_start(cst[:, P:n_const], consts[:, P:n_const]).then_inc(s_const, 16)
            for k in range(4, NK):
                load_first(k)
            for n in range(4):
                load_in(0, n)
            for s in range(2):
                load_mod(2, s, s)
            for L in range(DEPTH):
                if L > 0:
                    sp.wait_ge(s_o, L * NU)
                sp.dma_start(past[:, 0, :], cache_k[0, L].rearrange("t h d -> t (h d)")).then_inc(s_past, 16)
                sp.dma_start(past[:, 1, :], cache_v[0, L].rearrange("t h d -> t (h d)")).then_inc(s_past, 16)
                sp.dma_start(wp[:, :, :], w_pool[L].rearrange("g c d -> c g d")).then_inc(s_wp, 16)
                units_at = {0: (2, 3), 1: (4, 5), 2: (6,), 3: (7,)} if L == 0 else {}
                for n in range(N_IN):
                    if n + 4 < N_IN:
                        load_in(L, n + 4)
                    else:
                        load_out(L, n + 4 - N_IN)
                    for k in units_at.get(n, ()):
                        load_mod(2, k, k % 2)
                    if L == 0 and n in (4, 5):
                        load_mod(3, n - 4, n - 4)
                if L == 0:
                    for k in range(2, NK):
                        load_mod(3, k, k % 2)
                    for s in range(2):
                        load_mod(4, s, s)

                def load_up(j, L=L, g=0):
                    for s in range(2):
                        load_w(tile_up(L, g) + 2 * j + s, s,
                               w_up_v[L][:, :, ds(s * FF + (g * FG + j) * P, P)], NK)

                def load_down(i, L, g):
                    for s in range(2):
                        load_w(tile_down(L, g) + 2 * i + s, s,
                               w_down_v[L][:, g * FG:(g + 1) * FG, ds((2 * i + s) * P, P)], FG)

                for m in range(4):
                    load_out(L, 4 + m)
                    if L == 0 and m > 0:
                        for s in range(2):
                            load_mod(4, 2 * m + s, s)
                load_up(0, L, 0)
                for s in range(2):
                    load_mod(L * N_MOD + 5, s, s)
                load_up(1, L, 0)
                for g in range(NG):
                    A, B, C = mlp_chunks(L, g)
                    with sp.Fori(2, 5) as j:
                        load_up(j, L, g)
                        for s in range(2):
                            load_mod(A, 2 * j + (s - 2), s)
                    load_up(5, L, g)
                    for s in range(2):
                        load_mod(B, s, s)
                    load_up(6, L, g)
                    with sp.Fori(7, 10) as j:
                        load_up(j, L, g)
                        for s in range(2):
                            load_mod(B, 2 * j + (s - 12), s)
                    load_up(10, L, g)
                    load_down(0, L, g)
                    for s in range(2):
                        load_mod(C, s, s)
                    load_down(1, L, g)
                    for m in range(4):
                        load_w(tile_down(L, g) + 4 + m, m % 2,
                               w_down_v[L][:, g * FG:(g + 1) * FG, (4 + m) * P:(5 + m) * P], FG)
                        if m > 0:
                            for s in range(2):
                                load_mod(C, 2 * m + s, s)
                    if g + 1 < NG:
                        load_up(0, L, g + 1)
                        for s in range(2):
                            load_mod(mlp_chunks(L, g + 1)[0], s, s)
                        load_up(1, L, g + 1)
                    elif L + 1 < DEPTH:
                        for n in range(4):
                            load_in(L + 1, n)
            for b in range(NT):
                sp.wait_ge(s_yn, b + 1)
                dst = y_prompt[0] if b == 0 else y_sample[0, (b - 1) * P:b * P, :]
                sp.dma_start(dst, yout[:, b, :]).then_inc(s_out, 16)
            sp.wait_ge(s_out, 16 * (NT + 2 * DEPTH))

        @block.gpsimd
        def _(pool):
            pool.memset(eps[:, 0:1], EPS).then_inc(s_eps, 1)
            pool.memset(eps[:, 1:2], EPS / SCALE ** 2).then_inc(s_eps, 1)

            def clear_sum(i):
                if i > 0:
                    pool.wait_ge(s_stat, i)
                pool.memset(ssum[:, :], 0.0).then_inc(s_ss0, 1)

            def add_squares(i, m):
                if m == 0:
                    pool.wait_ge(s_ss0, i + 1)
                else:
                    pool.wait_ge(s_ss, i * (NK - 1) + m)
                pool.wait_ge(s_sq, i * NK + m + 1)
                pool.tensor_tensor(ssum[:, :], ssum[:, :], sq_slot(m), ALU.add).then_inc(s_ss, 1)

            def sq_slot(m):
                return sq[:, m % 2, :]

            clear_sum(0)
            for m in range(NK - 1):
                add_squares(0, m)
            for L in range(DEPTH):
                if L > 0:
                    pool.wait_ge(s_lin, tile_in(L))
                else:
                    pool.wait_ge(s_mfirst, NK)
                    pool.wait_ge(s_xe, NK)
                    pool.wait_ge(s_vec, DEPTH)
                for at in (0, U_P + TP, U_S + TS):
                    pool.memset(u[:, :, at:at + PAD], 0.0).then_inc(s_upad, 1)
                done = L * sum(range(1, NPOOL + 1))
                pool.wait_ge(s_upad, 3 * (L + 1))
                if L == 0:
                    pool.wait_ge(s_const, 16)
                for g in range(NPOOL):
                    pool.wait_ge(s_u, 2 * (L * NPOOL + g + 1))
                    src, lo, hi = u[:, g, :], 0, U_W
                    for r in range(g + 1):
                        left, right = (1, 0) if r == 0 else (2 ** (r - 1), 2 ** (r - 1))
                        lo, hi = lo + left, hi - right
                        dst = tree[:, r % 2, :]
                        if r == 0 and L * NPOOL + g > 0:
                            pool.wait_ge(s_pooled, L * NPOOL + g)
                        if r > 0:
                            pool.wait_ge(s_tstep, done)
                        pool.tensor_tensor(dst[:, lo:hi], src[:, lo - left:hi - left], src[:, lo + right:hi + right],
                                           ALU.add).then_inc(s_tstep, 1)
                        done += 1
                        src = dst
                    pool.wait_ge(s_tstep, done)
                    for s, (at, n) in enumerate(((U_P, TP), (U_S, TS))):
                        for e_, a0 in enumerate((at, at + n - PAD)):
                            pool.tensor_tensor(src[:, a0:a0 + PAD], src[:, a0:a0 + PAD], edge[:, g, s, e_, :],
                                               ALU.mult).then_inc(s_tree, 1)
                for e in range(NE):
                    E = L * NE + e
                    tgt = keys[:, TP + PAST:TP + PAST + TS] if e == 0 else qk[:, e % 3, TP:T]
                    if E > 0:
                        pool.wait_ge(s_qk, E)
                    pool.wait_ge(s_shuf, E + 1)
                    pool.tensor_tensor(rope[:, 1, :], rope[:, 0, :], sin, ALU.mult).then_inc(s_rp, 1)
                    pool.tensor_tensor(tgt, tgt, cos, ALU.mult).then_inc(s_rp, 1)
                    pool.wait_ge(s_rp, 2 * E + 2)
                    pool.tensor_tensor(tgt, tgt, rope[:, 1, :], ALU.add).then_inc(s_qk, 1)
                clear_sum(2 * L + 1)
                for m in range(NK - 1):
                    add_squares(2 * L + 1, m)
                for g in range(NG):
                    def gate(j, L=L, g=g):
                        n = (L * NG + g) * FG + j
                        pool.wait_ge(s_silu, n + 1)
                        pool.wait_ge(s_tap, 8 * n + 8)
                        pool.tensor_tensor(silu_a[:, :], silu_a[:, :], conv[:, 1, :], ALU.mult).then_inc(s_act, 1)
                        pool.wait_ge(s_act, n + 1)
                        pool.tensor_copy(act_hi[:, j, :], silu_a[:, :]).then_inc(s_ahi, 1)
                        pool.wait_ge(s_ahi, n + 1)
                        pool.tensor_tensor(act_lo[:, j, :], silu_a[:, :], act_hi[:, j, :].bitcast(F32),
                                           ALU.subtract).then_inc(s_alo, 1)
                    with pool.Fori(0, FG) as j:
                        gate(j)
                clear_sum(2 * L + 2)
                for m in range(NK - 1):
                    add_squares(2 * L + 2, m)

        @block.scalar
        def _(act_e):
            def hi(n, s, nk):
                act_e.wait_ge(s_raw[s], 16 * slot_loads(n, s))
                if not isinstance(n, int) or n >= 2:
                    act_e.wait_ge(s_lin, n - 1)
                act_e.activation(w_hi[:, s, 0:nk, :], w_raw[:, s, 0:nk, :], ACT.Copy).then_inc(s_whi, 1)

            def slot_loads(n, s):
                return n // 2 + 1 if isinstance(n, int) else (n - s) // 2 + 1

            def hi_third(n, nk, w):
                act_e.wait_ge(s_raw[0], 16 * slot_loads(n, 0))
                act_e.activation(w[:, 0:nk, :], w_raw[:, 0, 0:nk, :], ACT.Copy).then_inc(s_whi, 1)

            def hi_at(base, i, s, nk):
                act_e.wait_ge(s_raw[s], 16 * (i + (base // 2 + 1)))
                act_e.wait_ge(s_lin, 2 * i + (base + s - 1))
                act_e.activation(w_hi[:, s, 0:nk, :], w_raw[:, s, 0:nk, :], ACT.Copy).then_inc(s_whi, 1)

            def squares(i, upd, m):
                act_e.wait_ge(s_xupd, upd)
                if m >= 2:
                    act_e.wait_ge(s_ss, i * (NK - 1) + m - 1)
                else:
                    act_e.wait_ge(s_stat, i)
                act_e.activation(sq[:, m % 2, :], x[:, m, :], ACT.Square).then_inc(s_sq, 1)

            def std(i):
                act_e.wait_ge(s_stat, i + 1)
                act_e.activation(rtok[:, :], pair[3][:, 0:NT], ACT.Sqrt, bias=eps[:, 0:1], scale=1.0 / D).then_inc(s_sd, 1)

            def norm(i, L, which):
                std(i)
                act_e.wait_ge(s_mod, L * N_MOD + 3 * which + 1)
                for k in range(NK):
                    for ci, a, b in SEG:
                        act_e.wait_ge(s_nt, 2 * (i * NK + k) + 1 + ci)
                        act_e.activation(in_hi[:, k, a:b], norm_t[:, k % 2, a:b], ACT.Identity,
                                         bias=mod[:, L, 3 * which, ci, k:k + 1]).then_inc(s_hhi, 1)

            act_e.wait_ge(s_vec_t, 1)
            act_e.activation(cond[:, :, :].rearrange("p a b -> p (a b)"), pair[2][0:P, 0:2 * NK], ACT.Silu).then_inc(s_cond, 1)
            for L in range(DEPTH):
                act_e.wait_ge(s_vec_t, L + 2)
                for t in range(3):
                    ins = act_e.activation(vec[:, L, t, 0:N_ROWS[t]], pair[2][:, t * P:t * P + N_ROWS[t]], ACT.Copy)
                ins.then_inc(s_vec, 1)
            for k in range(NK):
                act_e.wait_ge(s_xt, k + 1)
                act_e.activation(x[:, k, :], pair[2 + k % 2][:, 0:T], ACT.Copy).then_inc(s_xe, 1)
                act_e.wait_ge(s_xe, k + 1)
                if k >= 2:
                    act_e.wait_ge(s_ss, k - 1)
                act_e.activation(sq[:, k % 2, :], x[:, k, :], ACT.Square).then_inc(s_sq, 1)
            for n in range(2):
                hi(n, n, NK)
            act_e.wait_ge(s_eps, 2)
            for L in range(DEPTH):
                norm(2 * L, L, 0)
                hi_third(tile_in(L) + 2, NK, w_third_in)

                def k_std():
                    act_e.wait_ge(s_qst, L * NE + 1)
                    act_e.activation(k_rstd[:, :], lin[3], ACT.Sqrt, bias=eps[:, 0:1], scale=1.0 / HD).then_inc(s_qsd, 1)

                def q_std():
                    act_e.wait_ge(s_qst, (L + 1) * NE)
                    act_e.activation(rq[:, 0, :], pair[3][:, 0:NQ * NT * 2], ACT.Sqrt, bias=eps[:, 1:2],
                                     scale=1.0 / (HD * SCALE ** 2)).then_inc(s_qsd, 1)

                def q_hi(e):
                    act_e.wait_ge(s_qk, L * NE + e + 1)
                    for i in range(2):
                        a = i * HALF
                        act_e.activation(q_st[a:a + HALF, 2 * (e - 1) + i, :], qk[a:a + HALF, e % 3, :],
                                         ACT.Copy).then_inc(s_qs_hi, 1)

                for n in range(N_IN):
                    N = tile_in(L) + n
                    act_e.wait_ge(s_lin, N + 1)
                    e = e_of(n)
                    if e is not None:
                        E = L * NE + e
                        if e >= 2:
                            act_e.wait_ge(s_qst, E - 1)
                        else:
                            act_e.wait_ge(s_stat, 2 * L + 1)
                        act_e.activation(sq[:, E % 2, :], lin[n % 2], ACT.Square).then_inc(s_qsq, 1)
                        if e == 3:
                            act_e.wait_ge(s_kn, L + 1)
                        elif e > 3:
                            act_e.wait_ge(s_qs, 2 * (L * NQ + e - 3))
                        if e == 0:
                            act_e.activation(qk[:, 0, :], lin[n % 2], ACT.Copy).then_inc(s_free, 1)
                        else:
                            act_e.activation(qk[:, e % 3, :], lin[n % 2], ACT.Copy, scale=v(L, V_QG, 0)).then_inc(s_free, 1)
                    elif n == IN_V:
                        act_e.activation(v_feat[:, :], lin[n % 2], ACT.Copy).then_inc(s_free, 1)
                    if N + 2 not in THIRD:
                        hi(N + 2, n % 2, NK)
                    if n == IN_K + 1:
                        k_std()
                    if n == IN_Q + 1:
                        act_e.wait_ge(s_vt, L + 1)
                        if L > 0:
                            act_e.wait_ge(s_out, 16 * 2 * L)
                            act_e.wait_ge(s_o, L * NU)
                        act_e.activation(val[:, :, :], pair[2][:, 0:T].rearrange("p (t c) -> p t c", t=NT),
                                         ACT.Copy).then_inc(s_val, 1)
                        act_e.activation(keys[:, TP:TP + PAST], pair[2][:, T:T + P], ACT.Copy).then_inc(s_pk, 1)
                        act_e.wait_ge(s_val, L + 1)
                        act_e.dma_start(new_v[0, L].rearrange("t h d -> t (h d)"), val[:, 0, :]).then_inc(s_out, 16)
                        act_e.wait_ge(s_qk, L * NE + 1)
                        act_e.wait_ge(s_pk, L + 1)
                        for g in range(KV // HD):
                            for a in (g * HALF, (1 - g) * HALF):
                                act_e.activation(k_hi[a:a + HALF, g, :], keys[g * HALF:(g + 1) * HALF, :],
                                                 ACT.Copy).then_inc(s_ks_hi, 1)
                    if n == IN_Q + 2:
                        act_e.wait_ge(s_kt, L + 1)
                        act_e.activation(k_out[:, :], pair[2][:, T:T + P], ACT.Copy).then_inc(s_kout, 1)
                        act_e.wait_ge(s_kout, L + 1)
                        act_e.dma_start(new_k[0, L].rearrange("t h d -> t (h d)"), k_out[:, :]).then_inc(s_out, 16)
                        q_hi(1)
                    if n == IN_Q + 3:
                        q_hi(2)
                for g in range(NPOOL):
                    act_e.wait_ge(s_pm, L * NPOOL + g + 1)
                    act_e.activation(in_hi[:, NQ + g, :], lin[g % 2], ACT.Copy,
                                     scale=v(L, V_PS, g)).then_inc(s_phi, 1)
                    if g == 1:
                        q_std()
                q_hi(3)
                for i in range(NU + 4):
                    if i < NU:
                        un = L * NU + i
                        nkeys = P if UNITS[i][0] == 0 else T
                        if i == 2:
                            q_hi(NQ)
                        act_e.wait_ge(s_neg, un + 1)
                        if i >= 3:
                            act_e.wait_ge(s_pt, un - 2)
                        act_e.activation(prob[i % 3][:, 0:nkeys], lin[i % 2][:, 0:nkeys], ACT.Exp,
                                         bias=small[:, i % 3, 0:1], scale=rq_of(0, i),
                                         accum_out=small[:, i % 3, 1:2]).then_inc(s_exp, 1)
                    if 2 <= i < NU + 2:
                        j = i - 2
                        nkeys = P if UNITS[j][0] == 0 else T
                        act_e.wait_ge(s_pt, L * NU + j + 1)
                        if j >= 2:
                            act_e.wait_ge(s_o, L * NU + j - 1)
                        act_e.activation(prob_t[:, j % 2, 0:nkeys], pair[2][:, 0:nkeys], ACT.Copy).then_inc(s_pte, 1)
                    if i >= 4 and (i - 3) % NH == 0:
                        pos = (i - 3) // NH - 1
                        b = BLOCKS[pos]
                        act_e.wait_ge(s_o, L * NU + (pos + 1) * NH)
                        act_e.activation(in_hi[:, 0:NQ, b * P:(b + 1) * P], o_bank(pos), ACT.Copy).then_inc(s_ohi, 1)
                up = tile_up(L, 0)
                out = tile_out(L)
                for m in range(N_OUT):
                    N = out + m
                    act_e.wait_ge(s_lin, N + 1)
                    hi(N + 2, m % 2, NK)
                    squares(2 * L + 1, upd_out(L) + m + 1, m)
                norm(2 * L + 1, L, 1)
                act_e.preload_act_table(ACT.Silu)
                for g in range(NG):
                    def up_iter(j, nxt, nk, L=L, g=g):
                        n = (L * NG + g) * FG + j
                        base = tile_up(L, g)
                        for s in range(2):
                            act_e.wait_ge(s_lin, 2 * j + (base + s + 1))
                            if L + g > 0 or not isinstance(j, int) or j > 0:
                                if s == 0:
                                    act_e.wait_ge(s_silu, n)
                                else:
                                    act_e.wait_ge(s_act, n)
                            act_e.activation(conv[:, s, :], up_result(g, j, s), ACT.Identity, bias=v(L, V_CONVB, s * NF + g * FG + j),
                                             scale=v(L, V_TAP[1], s * NF + g * FG + j)).then_inc(s_ctr, 1)
                            if isinstance(nxt, int):
                                if nxt + s not in THIRD:
                                    hi(nxt + s, s, nk)
                            else:
                                hi_at(base + 2, j, s, nk)
                        act_e.wait_ge(s_tap, 8 * n + 4)
                        if L + g > 0 or not isinstance(j, int) or j > 0:
                            act_e.wait_ge(s_alo, n)
                        act_e.activation(silu_a[:, :], conv[:, 0, :], ACT.Silu).then_inc(s_silu, 1)
                    if g == 0:
                        hi_third(tile_up(L, g) + 2, NK, w_third)
                    up_iter(0, tile_up(L, g) + 2, NK)
                    up_iter(1, tile_up(L, g) + 4, NK)
                    with act_e.Fori(2, FG - 1) as j:
                        up_iter(j, None, NK)
                    up_iter(FG - 1, tile_down(L, g), FG)

                    last = g == NG - 1 and L == DEPTH - 1
                    down = tile_down(L, g)
                    for m in range(NK):
                        N = down + m
                        act_e.wait_ge(s_lin, N + 1)
                        if N + 2 < DEPTH * PER_LAYER:
                            hi(N + 2, m % 2, FG if m + 2 < NK else NK)
                        if g == NG - 1:
                            squares(2 * L + 2, upd_down(L, g) + m + 1, m)
                            if L == DEPTH - 1:
                                if m >= 2:
                                    act_e.wait_ge(s_yt, m - 1)
                                act_e.activation(yf[:, m % 2, :], x[:, m, :], ACT.Copy,
                                                 scale=v(0, V_FIN, m)).then_inc(s_y, 1)
            std(2 * DEPTH)

        @block.vector
        def _(dve):
            def y_copy(m):
                dve.wait_ge(s_yt, m + 1)
                dve.tensor_copy(yout[:, :, m * P:(m + 1) * P],
                                pair[2 + m % 2][:, 0:T].rearrange("p (t c) -> p t c", t=NT)).then_inc(s_ye, 1)

            def o_low(L, pos):
                b = BLOCKS[pos]
                dve.wait_ge(s_ohi, L * NT + pos + 1)
                dve.tensor_tensor(in_lo[:, 0:NQ, b * P:(b + 1) * P], o_bank(pos),
                                  in_hi[:, 0:NQ, b * P:(b + 1) * P].bitcast(F32), ALU.subtract).then_inc(s_olo, 1)

            def lo(n, s, nk):
                dve.wait_ge(s_whi, n + 1)
                if isinstance(n, int) and n in THIRD:
                    dve.wait_ge(s_lin, n - 1)
                    w = w_third_in if n % PER_LAYER == 2 else w_third
                    dve.tensor_tensor(w_lo[:, s, 0:nk, :], w_raw[:, s, 0:nk, :], w[:, 0:nk, :].bitcast(F32),
                                      ALU.subtract).then_inc(s_wlo, 1)
                    return
                dve.tensor_tensor(w_lo[:, s, 0:nk, :], w_raw[:, s, 0:nk, :], w_hi[:, s, 0:nk, :].bitcast(F32),
                                  ALU.subtract).then_inc(s_wlo, 1)

            def mod_unit(C, k, s, conds=(0, 1)):
                if C is None:
                    return
                half = k // 2 if isinstance(k, int) else (k - s) // 2
                mod_unit_at(C, k, s, half, isinstance(k, int) and k == 0, conds)

            def mod_unit_at(C, k, s, half, first, conds=(0, 1)):
                if C is None:
                    return
                dve.wait_ge(s_mraw[s], 16 * half + 16 * (unit(C, 0) // 2 + 1))
                if first and C > 2:
                    dve.wait_ge(s_mred, C - 2)
                for ci in conds:
                    if first:
                        dve.tensor_scalar(mod_acc[:, ci, :], mod_raw[:, s, :], cond[:, ci, 0:1], None,
                                          ALU.mult).then_inc(s_macc, 1)
                    else:
                        dve.wait_ge(s_macc, 2 * k + (2 * unit(C, 0) + ci - 1))
                        dve.scalar_tensor_tensor(out=mod_acc[:, ci, :], in0=mod_raw[:, s, :],
                                                 scalar=cond[:, ci, ds(k, 1)], in1=mod_acc[:, ci, :],
                                                 op0=ALU.mult, op1=ALU.add).then_inc(s_macc, 1)

            def mod_finish(C):
                if C is None:
                    return
                L, ch = C // N_MOD, C % N_MOD
                if C < 2:
                    dve.wait_ge(s_mfirst, NK)
                else:
                    dve.wait_ge(s_mred, C - 1)
                for ci in range(2):
                    if C < 2:
                        sums = pair[C][:, :].rearrange("p (j i r) -> p i j r", j=NK, i=2)[:, ci, :, 0]
                    else:
                        sums = pair[2][:, MODP + ci * NK:MODP + (ci + 1) * NK]
                    ins = dve.tensor_tensor(mod[:, L, ch, ci, :], sums, v(L, V_BMOD, ch * NK, NK), ALU.add)
                ins.then_inc(s_mod, 1)
                if ch % 3 == 1:
                    dve.wait_ge(s_mod, C + 1)
                    for ci in range(2):
                        ins = dve.scalar_tensor_tensor(out=gain[:, L, ch // 3, ci, :], in0=mod[:, L, ch, ci, :],
                                                       scalar=1.0, in1=v(L, (V_N1, V_N2)[ch // 3], 0, NK),
                                                       op0=ALU.add, op1=ALU.mult)
                    ins.then_inc(s_gain, 1)

            def norm(i, L, which):
                dve.wait_ge(s_sd, i + 1)
                dve.reciprocal(rtok[:, :], rtok[:, :]).then_inc(s_rstd, 1)
                dve.wait_ge(s_bc, i + 1)
                dve.wait_ge(s_gain, 2 * L + which + 1)
                for k in range(NK + 1):
                    if k < NK:
                        for ci, a, b in SEG:
                            if k >= 2:
                                dve.wait_ge(s_h, 2 * (i * NK + k - 2) + 1 + ci)
                            dve.scalar_tensor_tensor(out=norm_t[:, k % 2, a:b], in0=x[:, k, a:b],
                                                     scalar=gain[:, L, which, ci, k:k + 1], in1=lin[3][:, a:b],
                                                     op0=ALU.mult, op1=ALU.mult).then_inc(s_nt, 1)
                    if k > 0:
                        for ci, a, b in SEG:
                            dve.wait_ge(s_hhi, 2 * (i * NK + k - 1) + 1 + ci)
                            dve.scalar_tensor_tensor(out=in_lo[:, k - 1, a:b], in0=norm_t[:, (k - 1) % 2, a:b],
                                                     scalar=mod[:, L, 3 * which, ci, k - 1:k],
                                                     in1=in_hi[:, k - 1, a:b].bitcast(F32),
                                                     op0=ALU.add, op1=ALU.subtract).then_inc(s_h, 1)

            def residual(N, s, L, ch, m):
                dve.wait_ge(s_lin, N + 1)
                for ci, a, b in SEG:
                    ins = dve.scalar_tensor_tensor(out=x[:, m, a:b], in0=lin[s][:, a:b],
                                                   scalar=mod[:, L, ch, ci, m:m + 1], in1=x[:, m, a:b],
                                                   op0=ALU.mult, op1=ALU.add)
                ins.then_inc(s_xupd, 1)

            for n in range(2):
                lo(n, n, NK)
            dve.wait_ge(s_vec, 1)
            for C in range(2):
                mod_finish(C)
            for L in range(DEPTH):
                norm(2 * L, L, 0)

                def k_norm():
                    dve.wait_ge(s_qsd, 2 * L + 1)
                    dve.reciprocal(k_rstd[:, :], k_rstd[:, :]).then_inc(s_qrs, 1)
                    dve.wait_ge(s_qrs, 2 * L + 1)
                    dve.wait_ge(s_free, L * (N_IN - NPOOL) + 1)
                    for d, a, b in ((keys[:, 0:TP], 0, TP), (keys[:, TP + PAST:], TP, T)):
                        ins = dve.scalar_tensor_tensor(out=d, in0=qk[:, 0, a:b], scalar=v(L, V_KG, 0),
                                                       in1=k_rstd[:, a:b], op0=ALU.mult, op1=ALU.mult)
                    ins.then_inc(s_kn, 1)
                    dve.wait_ge(s_kn, L + 1)

                def q_recip():
                    dve.wait_ge(s_qsd, 2 * L + 2)
                    dve.reciprocal(rq[:, 0, :], rq[:, 0, :]).then_inc(s_qrs, 1)
                    dve.wait_ge(s_qrs, 2 * L + 2)
                    dve.tensor_scalar(rq[:, 1, :], rq[:, 0, :], -1.0, None, ALU.mult).then_inc(s_nrq, 1)

                def shuffle(e):
                    E = L * NE + e
                    if e > 0:
                        dve.wait_ge(s_free, L * (N_IN - NPOOL) + E_TILE[e] - IN_K + 1)
                    if E > 0:
                        dve.wait_ge(s_rp, 2 * E)
                    latent = keys[:, TP + PAST:] if e == 0 else qk[:, e % 3, TP:T]
                    dve.stream_shuffle(rope[:, 0, :], latent, [(i + 16) % 32 for i in range(32)]).then_inc(s_shuf, 1)

                def q_low(e):
                    for i in range(2):
                        a, o = i * HALF, (1 - i) * HALF
                        dve.wait_ge(s_qs_hi, 2 * (L * NQ + e - 1) + i + 1)
                        dve.tensor_tensor(q_st[o:o + HALF, 2 * (e - 1) + i, :], qk[a:a + HALF, e % 3, :],
                                          q_st[a:a + HALF, 2 * (e - 1) + i, :].bitcast(F32),
                                          ALU.subtract).then_inc(s_qs, 1)

                def window_end(g):
                    dve.wait_ge(s_tree, 4 * (L * NPOOL + g + 1))
                    for at, n in ((U_P, TP), (U_S, TS)):
                        ins = dve.scalar_tensor_tensor(out=u[:, g, at:at + n], in0=tree[:, g % 2, at:at + n],
                                                       scalar=1.0 / WINDOWS[g], in1=u[:, g, at:at + n],
                                                       op0=ALU.mult, op1=ALU.subtract)
                    ins.then_inc(s_pooled, 1)

                def pool_low(g):
                    dve.wait_ge(s_phi, L * NPOOL + g + 1)
                    dve.scalar_tensor_tensor(out=in_lo[:, NQ + g, :], in0=lin[g % 2], scalar=v(L, V_PS, g),
                                             in1=in_hi[:, NQ + g, :].bitcast(F32), op0=ALU.mult,
                                             op1=ALU.subtract).then_inc(s_plo, 1)

                units_at = {0: (0, 1), 1: (2, 3), 2: (4,), 3: (5,), 4: (6,), 5: (7,)} if L == 0 else {}
                for n in range(N_IN):
                    N = tile_in(L) + n
                    dve.wait_ge(s_lin, N + 1)
                    if n < NPOOL:
                        if n == 0:
                            dve.wait_ge(s_upad, 3 * (L + 1))
                        src = lin[2 if n == 2 else n % 2]
                        dve.tensor_copy(u[:, n, U_P:U_P + TP], src[:, 0:TP]).then_inc(s_u, 1)
                        dve.tensor_copy(u[:, n, U_S:U_S + TS], src[:, TP:T]).then_inc(s_u, 1)
                    lo(N + 2, n % 2, NK)
                    if e_of(n - 1) is not None:
                        if e_of(n - 1) == 0:
                            k_norm()
                        shuffle(e_of(n - 1))
                    if 2 <= n < 2 + NPOOL:
                        window_end(n - 2)
                    if n == IN_Q + 1:
                        for g in range(KV // HD):
                            for i, a in enumerate((g * HALF, (1 - g) * HALF)):
                                dve.wait_ge(s_ks_hi, (L * 2 + g) * 2 + 1)
                                own = slice(g * HALF, (g + 1) * HALF)
                                dve.tensor_tensor(k_lo[a:a + HALF, g, :], keys[own, :], k_hi[own, g, :].bitcast(F32),
                                                  ALU.subtract).then_inc(s_ks, 1)
                    if n in (IN_Q + 2, IN_Q + 3):
                        q_low(n - IN_Q - 1)
                    for k in units_at.get(n, ()):
                        mod_unit(2, k, k % 2)
                for g in range(NPOOL):
                    pool_low(g)
                    if g == 0:
                        shuffle(NQ)
                    if g == 1:
                        q_recip()
                q_low(3)
                if L == 0:
                    mod_finish(2)
                for i in range(NU + 1):
                    if i < NU:
                        un = L * NU + i
                        nkeys = P if UNITS[i][0] == 0 else T
                        dve.wait_ge(s_s, un + 1)
                        dve.tensor_reduce(small[:, i % 3, 3:4], lin[i % 2][:, 0:nkeys], AX_X, ALU.max).then_inc(s_max, 1)
                        dve.wait_ge(s_max, un + 1)
                        if i >= 3:
                            dve.wait_ge(s_exp, un - 2)
                        if i == 0:
                            dve.wait_ge(s_nrq, L + 1)
                        dve.tensor_tensor(small[:, i % 3, 0:1], small[:, i % 3, 3:4], rq_of(1, i), ALU.mult)\
                           .then_inc(s_neg, 1)
                    if i > 0:
                        un, j = L * NU + i - 1, (i - 1) % 3
                        nkeys = P if UNITS[i - 1][0] == 0 else T
                        dve.wait_ge(s_exp, un + 1)
                        dve.reciprocal(small[:, j, 2:3], small[:, j, 1:2]).then_inc(s_rec, 1)
                        dve.wait_ge(s_rec, un + 1)
                        dve.tensor_scalar(prob[j][:, 0:nkeys], prob[j][:, 0:nkeys],
                                          small[:, j, 2:3], None, ALU.mult).then_inc(s_prob, 1)
                    if i == 2:
                        q_low(NQ)
                    if 5 <= i and (i - 4) % NH == 0:
                        o_low(L, (i - 4) // NH - 1)
                    if L == 0 and i % 2 == 0 and 4 <= i < 4 + 4 * NK:
                        k = i // 4 - 1
                        mod_unit(3, k, k % 2, (i % 4 // 2,))
                o_low(L, NT - 1)
                for m in range(N_OUT):
                    N = tile_out(L) + m
                    if m == 0:
                        dve.wait_ge(s_mod, L * N_MOD + 3)
                    residual(N, m % 2, L, 2, m)
                    lo(N + 2, m % 2, NK)
                    if L == 0 and m == 1:
                        mod_finish(3)
                    if L == 0 and 1 <= m <= 4:
                        for s in range(2):
                            mod_unit(4, 2 * (m - 1) + s, s)
                    if L == 0 and m == NK - 1:
                        mod_finish(4)
                norm(2 * L + 1, L, 1)
                for g in range(NG):
                    base = tile_up(L, g)

                    A, B, C = mlp_chunks(L, g)

                    def up_iter(j, nxt, nk, chunk=None, j0=0, L=L, g=g, base=base):
                        n = (L * NG + g) * FG + j
                        for s in range(2):
                            dve.wait_ge(s_ctr, 2 * n + s + 1)
                            tap = 4 * (2 * n + s)
                            for r, (t, sh) in enumerate(((0, -1), (2, 1))):
                                for ci, a, b in SEG:
                                    d0, d1 = (a + 1, b) if sh < 0 else (a, b - 1)
                                    if r == 1:
                                        dve.wait_ge(s_tap, tap + ci + 1)
                                    ins = dve.scalar_tensor_tensor(
                                        out=conv[:, s, d0:d1], in0=up_result(g, j, s)[:, d0 + sh:d1 + sh],
                                        scalar=v(L, V_TAP[t], s * NF + g * FG + j), in1=conv[:, s, d0:d1],
                                        op0=ALU.mult, op1=ALU.add).then_inc(s_tap, 1)
                            if isinstance(nxt, int):
                                lo(nxt + s, s, nk)
                            else:
                                lo(2 * j + (base + 2 + s), s, nk)
                            mod_unit_at(chunk, 2 * j + (s - 2 * j0), s, j - j0, isinstance(j, int) and j == j0 and s == 0)
                    up_iter(0, base + 2, NK, A)
                    up_iter(1, base + 4, NK, A)
                    with dve.Fori(2, 4) as j:
                        up_iter(j, None, NK, A)
                    up_iter(4, base + 10, NK)
                    mod_finish(A)
                    up_iter(5, base + 12, NK, B, 5)
                    with dve.Fori(6, 9) as j:
                        up_iter(j, None, NK, B, 5)
                    up_iter(9, base + 20, NK)
                    mod_finish(B)
                    up_iter(FG - 1, base + 2 * FG, FG)
                    down = tile_down(L, g)
                    dve.wait_ge(s_mod, (L + 1) * N_MOD)
                    for m in range(NK):
                        residual(down + m, m % 2, L, 5, m)
                        if down + m + 2 < DEPTH * PER_LAYER:
                            lo(down + m + 2, m % 2, FG if m + 2 < NK else NK)
                        if 1 <= m <= 4:
                            for s in range(2):
                                mod_unit(C, 2 * (m - 1) + s, s)
                        if m == NK - 1:
                            mod_finish(C)
                        if L == DEPTH - 1 and g == NG - 1 and m > 0:
                            y_copy(m - 1)
            y_copy(NK - 1)
            dve.wait_ge(s_sd, 2 * DEPTH + 1)
            dve.reciprocal(rtok[:, :], rtok[:, :]).then_inc(s_rstd, 1)
            dve.wait_ge(s_rstd, 2 * DEPTH + 1)
            dve.wait_ge(s_ye, NK)
            for b in range(NT):
                dve.tensor_scalar(yout[:, b, :], yout[:, b, :], rtok[:, b:b + 1], None, ALU.mult).then_inc(s_yn, 1)

        @block.tensor
        def _(pe):
            def split_matmul(dst, s, k, rhs_hi, rhs_lo, kk, first, last):
                passes = ((w_hi, rhs_hi), (w_hi, rhs_lo), (w_lo, rhs_hi))
                for r, (w, rhs) in enumerate(passes):
                    for hf in range(2):
                        a = hf * HALF_T
                        ins = pe.matmul(dst[:, a:a + HALF_T], w[:, s, k, :], rhs[:, kk, a:a + HALF_T],
                                        start=first and r == 0, stop=last and r == 2)
                return ins

            def linear(n, s, nk, rhs_hi, rhs_lo, dst=None, wait_k=None, order=None):
                pe.wait_ge(s_wlo, n + 1)
                order = list(order or range(nk))
                for k in order:
                    if wait_k is not None:
                        wait_k(k)
                    ins = split_matmul(lin[s] if dst is None else dst, s, k, rhs_hi, rhs_lo, k, k == order[0], k == order[-1])
                ins.then_inc(s_lin, 1)

            def product(dst, w, rhs, start, stop):
                for hf in range(2):
                    a = hf * HALF_T
                    ins = pe.matmul(dst[:, a:a + HALF_T], w, rhs[:, a:a + HALF_T], start=start, stop=stop)
                return ins

            def linear_pair(n, nk, rhs_hi, rhs_lo, wait_hi, wait_lo):
                pe.wait_ge(s_wlo, n + 2)
                for k in range(nk):
                    wait_hi(k)
                    for s in range(2):
                        product(lin[s], w_hi[:, s, k, :], rhs_hi[:, k, :], k == 0, False)
                        product(lin[s], w_lo[:, s, k, :], rhs_hi[:, k, :], False, False)
                    wait_lo(k)
                    for s in range(2):
                        ins = product(lin[s], w_hi[:, s, k, :], rhs_lo[:, k, :], False, k == nk - 1)
                        if k == nk - 1:
                            ins.then_inc(s_lin, 1)

            def linear_third(n, nk, rhs_hi, rhs_lo, dst, w):
                pe.wait_ge(s_whi, n + 1)
                for k in range(nk):
                    product(dst, w[:, k, :], rhs_hi[:, k, :], k == 0, False)
                    product(dst, w[:, k, :], rhs_lo[:, k, :], False, False)
                pe.wait_ge(s_wlo, n + 1)
                for k in range(nk):
                    ins = product(dst, w_lo[:, 0, k, :], rhs_hi[:, k, :], False, k == nk - 1)
                ins.then_inc(s_lin, 1)

            def stat(i, between=None):
                pe.wait_ge(s_ss, (i + 1) * (NK - 1))
                if i % 2 == 1:
                    pe.wait_ge(s_olo, (i // 2 + 1) * NT)
                for part, squares in enumerate((ssum[:, :], sq[:, (NK - 1) % 2, :])):
                    if part == 1:
                        if between is not None:
                            between()
                        pe.wait_ge(s_sq, (i + 1) * NK)
                    for b in range(NT):
                        ins = pe.matmul(pair[3][:, b:b + 1], squares[:, b * P:(b + 1) * P], ones[:, 0:1],
                                        start=part == 0 and b == 0, stop=part == 1, skip_group_check=True)
                ins.then_inc(s_stat, 1)

            def spread(i):
                pe.wait_ge(s_rstd, i + 1)
                for b in range(NT):
                    for lo_, hi_ in ((0, HALF_T), (HALF_T, T)):
                        a, e = max(b * P, lo_), min((b + 1) * P, hi_)
                        if a < e:
                            ins = pe.matmul(lin[3][:, a:e], rtok[:, b:b + 1].to_broadcast([P, P]),
                                            ident[:, a - b * P:e - b * P], start=True, stop=True)
                ins.then_inc(s_bc, 1)

            def mod_reduce(C, part=None):
                if C is None:
                    return
                if part != 1:
                    pe.wait_ge(s_macc, 2 * unit(C, NK))
                    pe.wait_ge(s_mod, C)
                for r in range(2 * NK) if part is None else range(part * NK, (part + 1) * NK):
                    ins = pe.matmul(pair[2][:, MODP + r:MODP + r + P], mod_acc[:, r // NK, (r % NK) * P:(r % NK + 1) * P],
                                    ones, start=True, stop=True)
                if part != 0:
                    ins.then_inc(s_mred, 1)

            def norm_stat(i, C):
                stat(i, lambda: mod_reduce(C, 0))
                mod_reduce(C, 1)
                spread(i)

            def y_transpose(m):
                pe.wait_ge(s_y, m + 1)
                if m >= 2:
                    pe.wait_ge(s_ye, m - 1)
                for b in range(NT):
                    ins = pe.transpose(pair[2 + m % 2][:, b * P:(b + 1) * P], yf[:, m % 2, b * P:(b + 1) * P], ident)
                ins.then_inc(s_yt, 1)

            def h_wait(i):
                return (lambda k: pe.wait_ge(s_hhi, 2 * (i * NK + k + 1)),
                        lambda k: pe.wait_ge(s_h, 2 * (i * NK + k + 1)))

            def mod_first(k):
                pe.wait_ge(s_first[k], 16)
                rhs = cond[:, :, k:k + 1].to_broadcast([P, 2, HALF])
                for j in range(2 * NK):
                    a = j % NK * P
                    ins = pe.matmul(pair[j // NK][:, a:a + P].rearrange("p (i r) -> p i r", i=2),
                                    w_first[:, k % N_FIRST, j * P:(j + 1) * P], rhs,
                                    start=k == 0 and j % 4 == 0, stop=k == NK - 1, skip_group_check=True)
                ins.then_inc(s_mfirst, 1)

            pe.wait_ge(s_const0, 16)
            pe.wait_ge(s_crow, 16 * 2)
            pe.transpose(pair[2][:, 0:2 * NK], cond_rows[:, :], ident[0:2 * NK, 0:2 * NK]).then_inc(s_vec_t, 1)
            pe.wait_ge(s_cond, 1)
            N_ROW_DMAS = 5 + 4 + 3 + DEPTH
            pe.wait_ge(s_rows, 16 * N_ROW_DMAS)
            for L in range(DEPTH):
                if L > 0:
                    pe.wait_ge(s_vec, L)
                for t in range(3):
                    ins = pe.transpose(pair[2][:, t * P:t * P + N_ROWS[t]], rows[0:N_ROWS[t], L, t, :],
                                       ident[0:N_ROWS[t], 0:N_ROWS[t]])
                ins.then_inc(s_vec_t, 1)
            for k in range(4):
                mod_first(k)
            pe.wait_ge(s_x, 32)
            pe.wait_ge(s_vec, DEPTH)
            for k in range(NK):
                if k >= 2:
                    pe.wait_ge(s_xe, k - 1)
                for b in range(NT):
                    ins = pe.transpose(pair[2 + k % 2][:, b * P:(b + 1) * P], xin[:, b, k * P:(k + 1) * P], ident)
                ins.then_inc(s_xt, 1)
            pe.wait_ge(s_const, 16)
            for k in range(4, NK):
                if k == NK - 1:
                    pe.wait_ge(s_xe, NK)
                    stat(0)
                mod_first(k)
            spread(0)

            def q_stat(E):
                pe.wait_ge(s_qsq, E + 1)
                if E % NE == 0:
                    for hf in range(2):
                        a = hf * HALF_T
                        ins = pe.matmul(lin[3][:, a:a + HALF_T], head_ones, sq[:, E % 2, a:a + HALF_T], start=True, stop=True)
                else:
                    if E % NE == 1:
                        pe.wait_ge(s_qsd, 2 * (E // NE) + 1)
                    for b in range(NT):
                        c = ((E % NE - 1) * NT + b) * 2
                        ins = pe.matmul(pair[3][:, c:c + 2], sq[:, E % 2, b * P:(b + 1) * P], head_ones[:, 0:P:HD],
                                        start=True, stop=True)
                ins.then_inc(s_qst, 1)

            for L in range(DEPTH):
                if L == 0:
                    pe.wait_ge(s_mod, 2)
                else:
                    pe.wait_ge(s_xupd, upd_down(L - 1, NG - 1) + NK)
                linear_pair(tile_in(L), NK, in_hi, in_lo, *h_wait(2 * L))
                linear_third(tile_in(L) + 2, NK, in_hi, in_lo, lin[2], w_third_in)
                for n in range(3, N_IN):
                    if n - 2 < IN_K:
                        pe.wait_ge(s_u, 2 * (L * NPOOL + n - 1))
                    else:
                        pe.wait_ge(s_free, L * (N_IN - NPOOL) + n - 1 - IN_K)
                    linear(tile_in(L) + n, n % 2, NK, in_hi, in_lo)
                    if n > 0 and e_of(n - 1) is not None:
                        q_stat(L * NE + e_of(n - 1))
                    if n == IN_Q:
                        pe.wait_ge(s_free, L * (N_IN - NPOOL) + IN_V - IN_K + 1)
                        pe.wait_ge(s_past, 32 * (L + 1))
                        for b in range(NT):
                            pe.transpose(pair[2][:, b * P:(b + 1) * P], v_feat[:, b * P:(b + 1) * P], ident)
                        pe.transpose(pair[2][:, T:T + P], past[:, 0, :], ident).then_inc(s_vt, 1)
                    if n == IN_Q + 2:
                        pe.wait_ge(s_pk, L + 1)
                        pe.wait_ge(s_kn, L + 1)
                        pe.transpose(pair[2][:, T:T + P], keys[:, 0:P], ident).then_inc(s_kt, 1)
                pe.wait_ge(s_wp, 16 * (L + 1))
                for g in range(NPOOL):
                    pe.wait_ge(s_pooled, L * NPOOL + g + 1)
                    if g < 2:
                        pe.wait_ge(s_free, L * (N_IN - NPOOL) + N_IN - 1 + g - IN_K)
                    else:
                        pe.wait_ge(s_plo, L * NPOOL + g - 1)
                    d = lin[g % 2]
                    pe.matmul(d[:, 0:TP], wp[:, g, :], u[:, g, U_P:U_P + TP], start=True, stop=True)
                    cut = HALF_T - TP
                    pe.matmul(d[:, TP:HALF_T], wp[:, g, :], u[:, g, U_S:U_S + cut], start=True, stop=True)
                    pe.matmul(d[:, HALF_T:T], wp[:, g, :], u[:, g, U_S + cut:U_S + TS], start=True,
                              stop=True).then_inc(s_pm, 1)
                    if g == 1:
                        q_stat(L * NE + NQ)
                if L == 0:
                    mod_reduce(2)

                def scores(i):
                    b, h = UNITS[i]
                    un = L * NU + i
                    if i < 2:
                        pe.wait_ge(s_plo, L * NPOOL + NPOOL - 1 + i)
                        pe.wait_ge(s_ks, 4 * (L + 1))
                    else:
                        pe.wait_ge(s_exp, un - 1)
                    pe.wait_ge(s_qs, 2 * L * NQ + h + 1)
                    runs = ((0, 0, 2 * P),) if b == 0 else tuple((TP + hf * HALF_T, hf * HALF_T, HALF_T) for hf in range(2))
                    for kc, oc, n in runs:
                        for r, kk in enumerate((k_hi, k_lo)):
                            ins = pe.matmul(lin[i % 2][:, oc:oc + n], q_st[:, h, b * P:(b + 1) * P],
                                            kk[:, h // GRP, kc:kc + n], start=r == 0, stop=r == 1)
                    ins.then_inc(s_s, 1)

                def transpose_prob(i):
                    un = L * NU + i
                    pe.wait_ge(s_prob, un + 1)
                    if i > 0:
                        pe.wait_ge(s_pte, un)
                    else:
                        pe.wait_ge(s_val, L + 1)
                        pe.wait_ge(s_kout, L + 1)
                    for kt in range(1 if UNITS[i][0] == 0 else NT):
                        ins = pe.transpose(pair[2][:, kt * P:(kt + 1) * P], prob[i % 3][:, kt * P:(kt + 1) * P], ident)
                    ins.then_inc(s_pt, 1)

                def weigh(i):
                    b, h = UNITS[i]
                    pos = i // NH
                    un = L * NU + i
                    a = (h % 2) * HALF
                    g = h // GRP
                    pe.wait_ge(s_pte, un + 1)
                    if h == 0:
                        if pos >= 2:
                            pe.wait_ge(s_olo, L * NT + pos - 1)
                        if pos == 0:
                            pe.wait_ge(s_qsd, 2 * (L + 1))
                    dst = pair[3][a:a + HALF, (pos % 2) * 512 + h // 2 * P:(pos % 2) * 512 + (h // 2 + 1) * P]
                    nkt = 1 if b == 0 else NT
                    for kt in range(nkt):
                        vv = val[:, 0, g * HD:(g + 1) * HD] if b == 0 else \
                            past[:, 1, g * HD:(g + 1) * HD] if kt == 0 else val[:, kt, g * HD:(g + 1) * HD]
                        ins = pe.matmul(dst, vv, prob_t[:, i % 2, kt * P:(kt + 1) * P], start=kt == 0, stop=kt == nkt - 1)
                    ins.then_inc(s_o, 1)

                scores(0)
                scores(1)
                for i in range(NU + 3):
                    if i >= 3:
                        weigh(i - 3)
                    if i + 2 < NU:
                        scores(i + 2)
                    if 1 <= i <= NU:
                        transpose_prob(i - 1)
                for i in range(2):
                    pe.wait_ge(s_exp, (L + 1) * NU - 1 + i)

                def out_wait(k):
                    if k == 0:
                        pe.wait_ge(s_olo, (L + 1) * NT)
                for m in range(N_OUT):
                    if m == 2 and L == 0:
                        mod_reduce(3)
                    if m >= 2:
                        pe.wait_ge(s_xupd, upd_out(L) + m - 1)
                    linear(tile_out(L) + m, m % 2, NK, in_hi, in_lo, wait_k=out_wait if m == 0 else None,
                           order=list(range(NQ, NK)) + list(range(NQ)))
                norm_stat(2 * L + 1, 4 if L == 0 else None)
                for g in range(NG):
                    base = tile_up(L, g)
                    A, B, C = mlp_chunks(L, g)

                    def up_iter(j, L=L, g=g, base=base):
                        for s in range(2):
                            pe.wait_ge(s_tap, 8 * j + (8 * (L * NG + g) * FG - 4 + 4 * s))
                            linear(2 * j + (base + s), s, NK, in_hi, in_lo)
                    if g == 0:
                        pe.wait_ge(s_xupd, upd_out(L) + NK)
                        linear_pair(base, NK, in_hi, in_lo, *h_wait(2 * L + 1))
                        pe.wait_ge(s_mod, L * N_MOD + 5)
                        linear_third(base + 2, NK, in_hi, in_lo, lin[2], w_third)
                        linear(base + 3, 1, NK, in_hi, in_lo, lin[3])
                    else:
                        for s in range(2):
                            pe.wait_ge(s_xupd, upd_down(L, g - 1) + NK - 1 + s)
                            linear(base + s, s, NK, in_hi, in_lo)
                        up_iter(1)
                    with pe.Fori(2, 5) as j:
                        up_iter(j)
                    mod_reduce(A)
                    with pe.Fori(5, FG - 1) as j:
                        up_iter(j)
                    mod_reduce(B)
                    up_iter(FG - 1)
                    down = tile_down(L, g)
                    done = (L * NG + g) * FG

                    last = L == DEPTH - 1 and g == NG - 1
                    for m in range(NK):
                        if m < 2:
                            pe.wait_ge(s_tap, 8 * (done + FG) - 4 * (1 - m))
                        else:
                            pe.wait_ge(s_xupd, upd_down(L, g) + m - 1)
                        linear(down + m, m % 2, FG, act_hi, act_lo,
                               wait_k=(lambda k: pe.wait_ge(s_alo, done + k + 1)) if m == 0 else None)
                        if last and m >= 2:
                            y_transpose(m - 2)
                    if not last:
                        if g == NG - 1:
                            norm_stat(2 * L + 2, C)
                        else:
                            mod_reduce(C)
            y_transpose(NK - 2)
            pe.wait_ge(s_ye, NK - 2)
            stat(2 * DEPTH)
            pe.wait_ge(s_sd, 2 * DEPTH + 1)
            y_transpose(NK - 1)


_INS = ['x_prompt', 'x_sample', 'cache_k', 'cache_v', 'c', 'c_ctx', 'w_mod', 'b_mod', 'norm1_g', 'w_in', 'q_norm_g',
        'k_norm_g', 'w_pool', 'pool_scale', 'w_out', 'norm2_g', 'w_up', 'conv_w', 'conv_b', 'w_down', 'final_norm_g']


def kernel(**inputs):
    import numpy as _np
    import concourse.bacc as _bacc
    from concourse import mybir as _mybir
    from concourse.bass_utils import run_bass_kernel_spmd as _run

    nc = _bacc.Bacc("TRN2", target_bir_lowering=False, num_devices=1)
    arrays, args = {}, []
    for name in _INS:
        arrays[f"in_{name}_dram"] = _np.ascontiguousarray(inputs[name])
    b, s, d = inputs['x_prompt'].shape
    db, ds_, _ = inputs['x_sample'].shape
    depth = inputs['w_in'].shape[0]
    kvh, hd = inputs['cache_k'].shape[3:]
    arrays["in_consts_dram"] = shape_constants(s, ds_, hd)
    for name, a in arrays.items():
        args.append(nc.dram_tensor(name, a.shape, _mybir.dt.from_np(a.dtype), kind="ExternalInput").ap())
    outs = [(b, s, d), (db, ds_, d), (b, depth, s, kvh, hd), (b, depth, s, kvh, hd)]
    for i, shape in enumerate(outs):
        args.append(nc.dram_tensor(f"out_{i}_dram", shape, _mybir.dt.float32, kind="ExternalOutput").ap())
    build(nc, *args)
    r = _run(nc, [arrays], core_ids=[0])
    return tuple(r.results[0][f"out_{i}_dram"] for i in range(len(outs)))
```
